# Optimizing a Trainium2 kernel written in Bass

```python
import math
import jax
import jax.numpy as jnp
from jax import lax
import numpy as np

D_MODEL = 1024
BATCH = 1
SEQ = 256
DEPTH = 2
DEC_BATCH = 8
DEC_SEQ = 1
PAST_LEN = 2048
PAGE_SIZE = 128

N_A_LAYERS = DEPTH // 2
N_B_LAYERS = DEPTH - N_A_LAYERS
ML_HEADS = 4
ML_DK = 128
ML_DV = 256
ML_CHUNK = 128
ML_IN_W = 2 * ML_HEADS * ML_DK + 2 * ML_HEADS * ML_DV + 2 * ML_HEADS
ML_FORGET_BIAS = 3.0
M_INIT = -1e30
MLA_HEADS = 8
NOPE_DIM = 128
ROPE_DIM = 64
V_DIM = 128
Q_LORA = 384
KV_LORA = 256
ROPE_THETA = 10000.0
Q_BLOCK = 128
N_EXPERTS = 64
TOP_K = 8
N_GROUPS = 8
TOPK_GROUPS = 4
EXPERT_FF = 256
SHARED_FF = 256
ROUTED_SCALE = 2.5
EXPERT_BLOCK = 128
NORM_EPS = 1e-6

kernel_name = 'yoco_mlstm_mla_moe_adaln_step'

def rmsnorm(x, g):
    xf = x.astype(jnp.float32)
    y = xf * lax.rsqrt(jnp.mean(xf * xf, axis=-1, keepdims=True) + NORM_EPS)
    return (y * g.astype(jnp.float32)).astype(x.dtype)

def modulate(h, shift, scale):
    return h * (1.0 + scale) + shift

def rope(x, pos):
    half = x.shape[-1] // 2
    inv = ROPE_THETA ** (-jnp.arange(half, dtype=jnp.float32) / half)
    ang = pos.astype(jnp.float32)[:, None] * inv[None, :]
    cos = jnp.cos(ang)[None, :, None, :]
    sin = jnp.sin(ang)[None, :, None, :]
    xf = x.astype(jnp.float32)
    x1, x2 = xf[..., :half], xf[..., half:]
    return jnp.concatenate([x1 * cos - x2 * sin, x2 * cos + x1 * sin], axis=-1).astype(x.dtype)

def mlstm_chunkwise(q, k, v, log_i, log_f, C0, n0, m0):
    B, T, H, _ = q.shape
    L = T if T <= ML_CHUNK else math.gcd(T, ML_CHUNK)
    nc = T // L
    causal = jnp.tril(jnp.ones((L, L), dtype=bool))

    def to_chunks(a):
        return a.reshape(B, nc, L, *a.shape[2:]).swapaxes(0, 1)

    def step(carry, inp):
        C, n, m = carry
        qc, kc, vc, ic, fc = inp
        b = jnp.cumsum(fc, axis=1)
        g = b + m[:, None, :]
        D = b[:, :, None, :] - b[:, None, :, :] + ic[:, None, :, :]
        D = jnp.where(causal[None, :, :, None], D, -jnp.inf)
        m_t = jnp.maximum(g, jnp.max(D, axis=2))
        w_intra = jnp.exp(D - m_t[:, :, None, :])
        w_inter = jnp.exp(g - m_t)
        s = jnp.einsum('bthd,bshd->btsh', qc, kc) * w_intra
        num = jnp.einsum('btsh,bshv->bthv', s, vc) + w_inter[..., None] * jnp.einsum('bthd,bhdv->bthv', qc, C)
        den = jnp.sum(s, axis=2) + w_inter * jnp.einsum('bthd,bhd->bth', qc, n)
        h = num / jnp.maximum(jnp.abs(den), jnp.exp(-m_t))[..., None]
        bL = b[:, -1, :]
        m_new = m_t[:, -1, :]
        a_inter = jnp.exp(bL + m - m_new)
        a_intra = jnp.exp(bL[:, None, :] - b + ic - m_new[:, None, :])
        C_new = a_inter[..., None, None] * C + jnp.einsum('bsh,bshd,bshv->bhdv', a_intra, kc, vc)
        n_new = a_inter[..., None] * n + jnp.einsum('bsh,bshd->bhd', a_intra, kc)
        return (C_new, n_new, m_new), h

    (C, n, m), hs = lax.scan(step, (C0, n0, m0),
                             (to_chunks(q), to_chunks(k), to_chunks(v), to_chunks(log_i), to_chunks(log_f)))
    return hs.swapaxes(0, 1).reshape(B, T, H, v.shape[-1]), C, n, m

def mlstm_mixer(h, w_in, b_gates, g_head, w_out, C0, n0, m0):
    B, T, _ = h.shape
    hk = ML_HEADS * ML_DK
    hv = ML_HEADS * ML_DV
    proj = h @ w_in
    q = proj[..., :hk].reshape(B, T, ML_HEADS, ML_DK).astype(jnp.float32)
    k = proj[..., hk:2 * hk].reshape(B, T, ML_HEADS, ML_DK).astype(jnp.float32) * (ML_DK ** -0.5)
    v = proj[..., 2 * hk:2 * hk + hv].reshape(B, T, ML_HEADS, ML_DV).astype(jnp.float32)
    o_gate = proj[..., 2 * hk + hv:2 * hk + 2 * hv]
    gates = (proj[..., 2 * hk + 2 * hv:] + b_gates).astype(jnp.float32)
    log_i = gates[..., :ML_HEADS]
    log_f = jax.nn.log_sigmoid(gates[..., ML_HEADS:])
    hh, C, n, m = mlstm_chunkwise(q, k, v, log_i, log_f, C0.astype(jnp.float32),
                                  n0.astype(jnp.float32), m0.astype(jnp.float32))
    hh = rmsnorm(hh, g_head.reshape(ML_HEADS, ML_DV)).reshape(B, T, hv)
    out = (hh.astype(h.dtype) * jax.nn.sigmoid(o_gate)) @ w_out
    return out, C, n, m

def shared_kv(x, cs, pos, w_ada_kv, b_ada_kv, g_kv_in, w_dkv, g_kv_lat):
    mod = (cs @ w_ada_kv + b_ada_kv)[:, None, :]
    sh, sc = jnp.split(mod, 2, axis=-1)
    h = modulate(rmsnorm(x, g_kv_in), sh, sc)
    ckr = h @ w_dkv
    lat = rmsnorm(ckr[..., :KV_LORA], g_kv_lat)
    kr = rope(ckr[..., None, KV_LORA:], pos)[:, :, 0, :]
    return lat, kr

def mla_attend(q_abs, q_rope, lat, kr, q_pos, k_pos):
    B, Tq, H, C = q_abs.shape
    qb = Q_BLOCK if Tq % Q_BLOCK == 0 else Tq
    nb = Tq // qb
    scale = (NOPE_DIM + ROPE_DIM) ** -0.5

    def split(a):
        return a.reshape(B, nb, qb, *a.shape[2:]).swapaxes(0, 1)

    def one_block(args):
        qa, qr, qp = args
        s = (jnp.einsum('bqhc,bkc->bhqk', qa, lat) + jnp.einsum('bqhr,bkr->bhqk', qr, kr)).astype(jnp.float32) * scale
        mask = k_pos[None, :] <= qp[:, None]
        p = jax.nn.softmax(jnp.where(mask[None, None], s, -jnp.inf), axis=-1).astype(lat.dtype)
        return jnp.einsum('bhqk,bkc->bqhc', p, lat)

    o = lax.map(one_block, (split(q_abs), split(q_rope), q_pos.reshape(nb, qb)))
    return o.swapaxes(0, 1).reshape(B, Tq, H, C)

def mla_mixer(h, pos, k_pos, lat, kr, w_dq, g_q_lat, w_uq, w_uk, w_uv, w_out):
    B, T, _ = h.shape
    q_lat = rmsnorm(h @ w_dq, g_q_lat)
    q = (q_lat @ w_uq).reshape(B, T, MLA_HEADS, NOPE_DIM + ROPE_DIM)
    q_rope = rope(q[..., NOPE_DIM:], pos)
    q_abs = jnp.einsum('bthn,chn->bthc', q[..., :NOPE_DIM], w_uk)
    o_lat = mla_attend(q_abs, q_rope, lat, kr, pos, k_pos)
    o = jnp.einsum('bthc,chv->bthv', o_lat, w_uv).reshape(B, T, MLA_HEADS * V_DIM)
    return o @ w_out

def swiglu(x, w_gate, w_up, w_down):
    return (jax.nn.silu(x @ w_gate) * (x @ w_up)) @ w_down

def routed_experts(xf, idx, wts, w_gate, w_up, w_down):
    n_tok, d = xf.shape
    n_assign = n_tok * TOP_K
    n_blocks = (n_assign + N_EXPERTS * (EXPERT_BLOCK - 1) + EXPERT_BLOCK - 1) // EXPERT_BLOCK
    n_rows = n_blocks * EXPERT_BLOCK
    flat_e = idx.reshape(-1)
    flat_tok = jnp.arange(n_assign, dtype=jnp.int32) // TOP_K
    flat_w = wts.reshape(-1)
    order = jnp.argsort(flat_e)
    e_s = flat_e[order]
    counts = jnp.bincount(flat_e, length=N_EXPERTS)
    padded = (counts + EXPERT_BLOCK - 1) // EXPERT_BLOCK * EXPERT_BLOCK
    pad_end = jnp.cumsum(padded)
    pad_start = pad_end - padded
    unpad_start = jnp.cumsum(counts) - counts
    dest = pad_start[e_s] + jnp.arange(n_assign, dtype=jnp.int32) - unpad_start[e_s]
    row_tok = jnp.full((n_rows,), n_tok, jnp.int32).at[dest].set(flat_tok[order])
    row_w = jnp.zeros((n_rows,), xf.dtype).at[dest].set(flat_w[order].astype(xf.dtype))
    block_start = jnp.arange(n_blocks, dtype=jnp.int32) * EXPERT_BLOCK
    block_e = jnp.minimum(jnp.searchsorted(pad_end, block_start, side='right'), N_EXPERTS - 1)
    x_pad = jnp.concatenate([xf, jnp.zeros((1, d), xf.dtype)], axis=0)

    def one_block(args):
        tok, w, e = args
        xb = x_pad[tok]
        hb = jax.nn.silu(xb @ w_gate[e]) * (xb @ w_up[e])
        return (hb @ w_down[e]) * w[:, None]

    out = lax.map(one_block, (row_tok.reshape(n_blocks, EXPERT_BLOCK), row_w.reshape(n_blocks, EXPERT_BLOCK), block_e))
    return jax.ops.segment_sum(out.reshape(n_rows, d), row_tok, num_segments=n_tok + 1)[:n_tok]

def moe(h, w_router, b_router, w_gate, w_up, w_down, ws_gate, ws_up, ws_down):
    shp = h.shape
    xf = h.reshape(-1, shp[-1])
    n_tok = xf.shape[0]
    scores = jax.nn.sigmoid((xf @ w_router).astype(jnp.float32))
    sel = scores + b_router.astype(jnp.float32)
    grp = sel.reshape(n_tok, N_GROUPS, N_EXPERTS // N_GROUPS)
    gscore = jnp.sum(lax.top_k(grp, 2)[0], axis=-1)
    _, gidx = lax.top_k(gscore, TOPK_GROUPS)
    gmask = jnp.sum(jax.nn.one_hot(gidx, N_GROUPS, dtype=jnp.float32), axis=1) > 0
    sel = jnp.where(jnp.repeat(gmask, N_EXPERTS // N_GROUPS, axis=1), sel, -jnp.inf)
    _, idx = lax.top_k(sel, TOP_K)
    wts = jnp.take_along_axis(scores, idx, axis=1)
    wts = wts / jnp.sum(wts, axis=-1, keepdims=True) * ROUTED_SCALE
    routed = routed_experts(xf, idx, wts, w_gate, w_up, w_down)
    shared = swiglu(xf, ws_gate, ws_up, ws_down)
    return (routed + shared).reshape(shp)

def run_group(x, c, pos0, C0s, n0s, m0s, past_lat, past_kr, p):
    B, T, _ = x.shape
    pos = pos0 + jnp.arange(T, dtype=jnp.int32)
    k_pos = jnp.arange(past_lat.shape[1] + T, dtype=jnp.int32)
    cs = jax.nn.silu(c)
    Cs, ns, ms = [], [], []
    lat_all = kr_all = new_lat = new_kr = None
    for l in range(DEPTH):
        mod = (cs @ p['w_ada'][l] + p['b_ada'][l])[:, None, :]
        sh_m, sc_m, g_m, sh_f, sc_f, g_f = jnp.split(mod, 6, axis=-1)
        h = modulate(rmsnorm(x, p['g_mix'][l]), sh_m, sc_m)
        if l < N_A_LAYERS:
            out, Cn, nn_, mn = mlstm_mixer(h, p['w_mlstm_in'][l], p['b_mlstm_gates'][l], p['g_mlstm_head'][l],
                                           p['w_mlstm_out'][l], C0s[l], n0s[l], m0s[l])
            Cs.append(Cn)
            ns.append(nn_)
            ms.append(mn)
        else:
            if l == N_A_LAYERS:
                new_lat, new_kr = shared_kv(x, cs, pos, p['w_ada_kv'], p['b_ada_kv'], p['g_kv_in'],
                                            p['w_dkv'], p['g_kv_lat'])
                lat_all = jnp.concatenate([past_lat.astype(new_lat.dtype), new_lat], axis=1)
                kr_all = jnp.concatenate([past_kr.astype(new_kr.dtype), new_kr], axis=1)
            j = l - N_A_LAYERS
            out = mla_mixer(h, pos, k_pos, lat_all, kr_all, p['w_dq'][j], p['g_q_lat'][j], p['w_uq'][j],
                            p['w_uk'], p['w_uv'], p['w_mla_out'][j])
        x = x + g_m * out
        h = modulate(rmsnorm(x, p['g_ffn'][l]), sh_f, sc_f)
        x = x + g_f * moe(h, p['w_router'][l], p['b_router'][l], p['w_exp_gate'][l], p['w_exp_up'][l],
                          p['w_exp_down'][l], p['w_sh_gate'][l], p['w_sh_up'][l], p['w_sh_down'][l])
    y = rmsnorm(x, p['g_final'])
    return y, jnp.stack(Cs), jnp.stack(ns), jnp.stack(ms), new_lat, new_kr

def setup_inputs(seed: int = 0) -> dict:
    key = jax.random.key(seed)
    ks = iter(jax.random.split(key, 64))

    def nrm(shape, scale):
        return jax.random.normal(next(ks), shape, jnp.float32) * scale

    def gain(shape):
        return 1.0 + nrm(shape, 0.05)

    n_pages = PAST_LEN // PAGE_SIZE
    n_phys = (5 * DEC_BATCH * n_pages) // 4
    page_table = jax.random.permutation(next(ks), n_phys)[:DEC_BATCH * n_pages].reshape(DEC_BATCH, n_pages).astype(jnp.int32)
    D = D_MODEL
    b_gates = jnp.concatenate([nrm((N_A_LAYERS, ML_HEADS), 0.1),
                               ML_FORGET_BIAS + nrm((N_A_LAYERS, ML_HEADS), 0.1)], axis=-1)
    return {
        'x_prompt': nrm((BATCH, SEQ, D), 1.0),
        'x_sample': nrm((DEC_BATCH, DEC_SEQ, D), 1.0),
        'state_mlstm_C': nrm((N_A_LAYERS, DEC_BATCH, ML_HEADS, ML_DK, ML_DV), 0.1),
        'state_mlstm_n': nrm((N_A_LAYERS, DEC_BATCH, ML_HEADS, ML_DK), 0.1),
        'state_mlstm_m': nrm((N_A_LAYERS, DEC_BATCH, ML_HEADS), 1.0),
        'cache_latent': nrm((n_phys, PAGE_SIZE, KV_LORA), 1.0),
        'cache_krope': nrm((n_phys, PAGE_SIZE, ROPE_DIM), 1.0),
        'page_table': page_table,
        'c_prompt': nrm((BATCH, D), 1.0),
        'c_sample': nrm((DEC_BATCH, D), 1.0),
        'w_ada': nrm((DEPTH, D, 6 * D), 0.5 * D ** -0.5),
        'b_ada': nrm((DEPTH, 6 * D), 0.02),
        'g_mix': gain((DEPTH, D)),
        'g_ffn': gain((DEPTH, D)),
        'w_mlstm_in': nrm((N_A_LAYERS, D, ML_IN_W), D ** -0.5),
        'b_mlstm_gates': b_gates,
        'g_mlstm_head': gain((N_A_LAYERS, ML_HEADS * ML_DV)),
        'w_mlstm_out': nrm((N_A_LAYERS, ML_HEADS * ML_DV, D), (ML_HEADS * ML_DV) ** -0.5),
        'w_ada_kv': nrm((D, 2 * D), 0.5 * D ** -0.5),
        'b_ada_kv': nrm((2 * D,), 0.02),
        'g_kv_in': gain((D,)),
        'w_dkv': nrm((D, KV_LORA + ROPE_DIM), D ** -0.5),
        'g_kv_lat': gain((KV_LORA,)),
        'w_uk': nrm((KV_LORA, MLA_HEADS, NOPE_DIM), KV_LORA ** -0.5),
        'w_uv': nrm((KV_LORA, MLA_HEADS, V_DIM), KV_LORA ** -0.5),
        'w_dq': nrm((N_B_LAYERS, D, Q_LORA), D ** -0.5),
        'g_q_lat': gain((N_B_LAYERS, Q_LORA)),
        'w_uq': nrm((N_B_LAYERS, Q_LORA, MLA_HEADS * (NOPE_DIM + ROPE_DIM)), Q_LORA ** -0.5),
        'w_mla_out': nrm((N_B_LAYERS, MLA_HEADS * V_DIM, D), (MLA_HEADS * V_DIM) ** -0.5),
        'w_router': nrm((DEPTH, D, N_EXPERTS), D ** -0.5),
        'b_router': nrm((DEPTH, N_EXPERTS), 0.01),
        'w_exp_gate': nrm((DEPTH, N_EXPERTS, D, EXPERT_FF), D ** -0.5),
        'w_exp_up': nrm((DEPTH, N_EXPERTS, D, EXPERT_FF), D ** -0.5),
        'w_exp_down': nrm((DEPTH, N_EXPERTS, EXPERT_FF, D), EXPERT_FF ** -0.5),
        'w_sh_gate': nrm((DEPTH, D, SHARED_FF), D ** -0.5),
        'w_sh_up': nrm((DEPTH, D, SHARED_FF), D ** -0.5),
        'w_sh_down': nrm((DEPTH, SHARED_FF, D), SHARED_FF ** -0.5),
        'g_final': gain((D,)),
    }

def reference(x_prompt, x_sample, state_mlstm_C, state_mlstm_n, state_mlstm_m, cache_latent, cache_krope,
              page_table, c_prompt, c_sample, w_ada, b_ada, g_mix, g_ffn, w_mlstm_in, b_mlstm_gates,
              g_mlstm_head, w_mlstm_out, w_ada_kv, b_ada_kv, g_kv_in, w_dkv, g_kv_lat, w_uk, w_uv, w_dq,
              g_q_lat, w_uq, w_mla_out, w_router, b_router, w_exp_gate, w_exp_up, w_exp_down, w_sh_gate,
              w_sh_up, w_sh_down, g_final):
    p = dict(w_ada=w_ada, b_ada=b_ada, g_mix=g_mix, g_ffn=g_ffn, w_mlstm_in=w_mlstm_in,
             b_mlstm_gates=b_mlstm_gates, g_mlstm_head=g_mlstm_head, w_mlstm_out=w_mlstm_out,
             w_ada_kv=w_ada_kv, b_ada_kv=b_ada_kv, g_kv_in=g_kv_in, w_dkv=w_dkv, g_kv_lat=g_kv_lat,
             w_uk=w_uk, w_uv=w_uv, w_dq=w_dq, g_q_lat=g_q_lat, w_uq=w_uq, w_mla_out=w_mla_out,
             w_router=w_router, b_router=b_router, w_exp_gate=w_exp_gate, w_exp_up=w_exp_up,
             w_exp_down=w_exp_down, w_sh_gate=w_sh_gate, w_sh_up=w_sh_up, w_sh_down=w_sh_down,
             g_final=g_final)
    C0 = jnp.zeros((N_A_LAYERS, BATCH, ML_HEADS, ML_DK, ML_DV), jnp.float32)
    n0 = jnp.zeros((N_A_LAYERS, BATCH, ML_HEADS, ML_DK), jnp.float32)
    m0 = jnp.full((N_A_LAYERS, BATCH, ML_HEADS), M_INIT, jnp.float32)
    empty_lat = jnp.zeros((BATCH, 0, KV_LORA), x_prompt.dtype)
    empty_kr = jnp.zeros((BATCH, 0, ROPE_DIM), x_prompt.dtype)
    y_prompt, p_C, p_n, p_m, p_lat, p_kr = run_group(x_prompt, c_prompt, 0, C0, n0, m0, empty_lat, empty_kr, p)
    n_pages = PAST_LEN // PAGE_SIZE
    past_lat = cache_latent[page_table].reshape(DEC_BATCH, n_pages * PAGE_SIZE, KV_LORA)
    past_kr = cache_krope[page_table].reshape(DEC_BATCH, n_pages * PAGE_SIZE, ROPE_DIM)
    y_sample, s_C, s_n, s_m, s_lat, s_kr = run_group(x_sample, c_sample, PAST_LEN, state_mlstm_C, state_mlstm_n,
                                                     state_mlstm_m, past_lat, past_kr, p)
    return (y_prompt, y_sample, p_C, p_n, p_m, p_lat, p_kr, s_C, s_n, s_m, s_lat, s_kr)


_drawn_inputs = setup_inputs


def setup_inputs(seed=0):
    import zlib

    import numpy as np

    out = dict(_drawn_inputs(seed))
    spreads = {}
    factors = {'cache_latent': 5.602, 'cache_krope': 8.0, 'g_q_lat': 4.924}
    for name, (base, spread) in spreads.items():
        noise = np.random.default_rng([zlib.crc32(name.encode()), seed]).standard_normal(out[name].shape)
        drawn = base * np.exp(spread * noise) if base else spread * noise
        out[name] = jnp.asarray(drawn.astype(out[name].dtype))
    for name, factor in factors.items():
        out[name] = (out[name] * factor).astype(out[name].dtype)
    return out
```

```python
from contextlib import ExitStack

import numpy as np

import concourse.bass as bass
from concourse import mybir

ALU = mybir.AluOpType
ACT = mybir.ActivationFunctionType
F32 = mybir.dt.float32
I32 = mybir.dt.int32
AX_X = mybir.AxisListType.X

P = 128
D = 1024
KC = D // P
TP = 256
TS = 8
T = TP + TS
TPAD = 3 * P
H = 4
DK, DV = 128, 256
L = 128
VA = DV + 1
AH = 8
NOPE, ROPE, VD = 128, 64, 128
QL, CL = 384, 256
PAGES, PAGE = 16, 128
E = 64
FF = 256
EPS = 1e-6
M_INIT = -1e30
NEG = -1e30
ROUTED_SCALE = 2.5
ATT_SCALE = float(NOPE + ROPE) ** -0.5
NMOD = 2 * 48 + 16
RING = 6
TILE = 2048
SLOTS = 64
NBLK = 98
MAXOVER = 32

C_ID, C_STRIU, C_TRIU, C_CAUS, C_ONES = 0, 128, 256, 384, 512
C_SEL = 640
C_IOTA = C_SEL + 4 * 128
C_COS = C_IOTA + 64
C_SIN = C_COS + T
C_ROT = C_SIN + T
C_VALID = C_ROT + 64
C_EPS = C_VALID + 3
C_SELF = C_EPS + 1
C_PMOD = C_SELF + 8
C_TOK = C_PMOD + 1
NCONST = C_TOK + 3


def constants():
    c = np.zeros((P, NCONST), np.float32)
    i = np.arange(P)
    c[:, C_ID:C_ID + P] = np.eye(P)
    c[:, C_STRIU:C_STRIU + P] = i[:, None] < i[None, :]
    c[:, C_TRIU:C_TRIU + P] = i[:, None] <= i[None, :]
    c[:, C_CAUS:C_CAUS + P] = np.where(i[None, :] <= i[:, None], 0.0, NEG)
    c[:, C_ONES:C_ONES + P] = 1.0
    for h in range(H):
        c[h, C_SEL + h * P:C_SEL + (h + 1) * P] = 1.0
    c[:, C_IOTA:C_IOTA + 64] = np.arange(64)[None, :]
    half = ROPE // 2
    inv = (np.float32(10000.0) ** (-np.arange(half, dtype=np.float32) / half)).astype(np.float32)
    pos = np.concatenate([np.arange(TP), np.full(TS, PAGES * PAGE)]).astype(np.float32)
    ang = (pos[None, :] * inv[:, None]).astype(np.float32).astype(np.float64)
    c[0:64, C_COS:C_COS + T] = np.concatenate([np.cos(ang), np.cos(ang)])
    c[0:64, C_SIN:C_SIN + T] = np.concatenate([np.sin(ang), np.sin(ang)])
    for m in range(half):
        c[m + half, C_ROT + m] = -1.0
        c[m, C_ROT + m + half] = 1.0
    c[:, C_VALID:C_VALID + 2] = 1.0
    c[0:TS, C_VALID + 2] = 1.0
    c[:, C_EPS] = EPS
    c[:, C_SELF:C_SELF + 8] = np.where(np.eye(P, 8) > 0, 0.0, NEG)
    c[:, C_PMOD] = i % 8
    c[:, C_TOK:C_TOK + 3] = i[:, None] + P * np.arange(3)[None, :]
    return c


class Chain:

    def __init__(self, eng, sem, base=0):
        self.eng, self.sem, self.base, self.n = eng, sem, base, 0

    def step(self, ins):
        self.n += 1
        ins.then_inc(self.sem, 1)
        self.eng.wait_ge(self.sem, self.base + self.n)

    def mark(self, ins):
        self.n += 1
        ins.then_inc(self.sem, 1)


def rep(ap, axis, n):
    a = ap.unsqueeze(axis)
    shape = list(a.shape)
    shape[axis] = n
    return a.to_broadcast(shape)


def decoder_step(nc, a, outs):
    (y_p, y_s, o_pC, o_pn, o_pm, o_plat, o_pkr, o_sC, o_sn, o_sm, o_slat, o_skr) = outs
    ctx = ExitStack()
    with ctx:
        def sb(name, shape, dt=F32):
            return ctx.enter_context(nc.sbuf_tensor(name, shape, dt))

        NORM = {tag: n + 1 for n, tag in enumerate(("mix0", "head", "ffn0", "mix1", "lat", "ql", "ffn1", "fin"))}
        H_READY = {tag: n + 1 for n, tag in enumerate(("mix0", "ffn0", "kv", "mix1", "ffn1"))}
        sems = {}

        def ev(name):
            if name not in sems:
                sems[name] = ctx.enter_context(nc.semaphore("s_" + name))
            return sems[name]

        h_rows = nc.dram_tensor("h_rows", [T, D], F32, kind="Internal").ap()
        slot_token = nc.dram_tensor("slot_token", [SLOTS * NBLK, 1], I32, kind="Internal").ap()
        y_slots = nc.dram_tensor("y_slots", [SLOTS * (E + MAXOVER), D], F32, kind="Internal").ap()

        ps = ctx.enter_context(nc.psum_tensor("ps", [P, 8, 512], F32))
        ring = sb("ring", [P, RING, TILE])
        cst = sb("cst", [P, NCONST])
        xT = sb("xT", [P, KC, T])
        hT = sb("hT", [P, KC, TPAD])
        xn = sb("xn", [P, KC, T])
        rs = sb("rs", [P, 4, T])
        modT = sb("modT", [P, NMOD, 9])
        colA = sb("colA", [P, 112])
        colB = sb("colB", [P, 61])
        csT = sb("csT", [P, KC, 9])
        amod = sb("amod", [P, KC, 9])
        wrt = sb("wrt", [P, 2, KC, E])
        brt = sb("brt", [P, 2, E])
        small = sb("small", [P, 512])
        niter = sb("niter", [1, 2], I32)
        blk_e = sb("blk_e", [1, 2, E], I32)
        tok_i = sb("tok_i", [P, 3], I32)
        zero_i = sb("zero_i", [SLOTS, NBLK], I32)
        zero_row = sb("zero_row", [P, 512])
        arena = sb("arena", [P, 26900])

        ident = cst[:, C_ID:C_ID + P]
        ones = cst[:, C_ONES:C_ONES + P]
        eps_col = cst[:, C_EPS:C_EPS + 1]
        one_col = cst[:, C_ONES:C_ONES + 1]
        B_MIX, B_FFN, B_KV, B_FIN, B_HEAD, B_LAT, B_QL = 0, 16, 32, 40, 48, 56, 58

        def carve():
            at = [0]

            def take(*shape, parts=P, dt=F32):
                n = int(np.prod(shape))
                v = arena[0:parts, at[0]:at[0] + n]
                at[0] += n
                assert at[0] <= 26900, at[0]
                if dt is not F32:
                    v = v.bitcast(dt)
                if len(shape) > 1:
                    names = "abcd"[:len(shape)]
                    v = v.rearrange(f"p ({' '.join(names)}) -> p {' '.join(names)}",
                                    **{k: s for k, s in zip(names, shape)})
                return v
            return take

        take = carve()
        x_rows = take(3, D)
        c_rows = take(D)
        c_sig = take(D)
        rowA = take(P)
        rowB = take(P)

        take = carve()
        projT = take(24, T)
        k_tok = take(2, H * DK)
        v_tok = take(2, H, VA)
        c_half = take(16, DV)
        hh = take(KC, T)
        wmat = take(2, L)
        smat = take(2, L)
        ka = take(2, DK)
        c1 = take(VA)
        qw = take(L)
        nb = take(P)
        enm = take(2 * L)
        mlx = take(2 * L)
        wg = take(KC, 8)
        gr = take(12, 2 * L, parts=H)
        scan = take(2, 2, 192, parts=H)
        rowsS = take(16, 8, parts=H)
        row_wi = take(L + 24, parts=H)
        smp = take(24, H * TS)
        bcs = take(H, 24)
        nrow = take(P)
        mod_rows = arena[0:9, 0:6 * D]
        rows_s = hT[0:TS].rearrange("p c n -> p (c n)")
        k_one = rows_s[:, 0:H * DK]
        k_row = rows_s[:, H * DK:2 * H * DK]
        v_row = rows_s[:, 2 * H * DK:2 * H * DK + H * DV]

        def tile_k(w, c0, n):
            return w.rearrange("(k p) n -> p k n", p=P)[:, :, c0:c0 + n]

        def slot(s, k, n):
            return ring[:, s, 0:k * n].rearrange("p (k n) -> p k n", k=k)

        w_in, w_out = a["w_mlstm_in"][0], a["w_mlstm_out"][0]
        NADA = 24
        straight_a = [(tile_k(a["w_ada_kv"], i * 256, 256), KC, 256) for i in range(8)]
        straight_a += [(tile_k(w_in, i * 256, 256), KC, 256) for i in range(12)]
        straight_a += [(tile_k(w_out, i * 256, 256), KC, 256) for i in range(4)]

        def shared_tiles(l):
            return [(tile_k(a["w_sh_gate"][l], 0, FF), KC, FF), (tile_k(a["w_sh_up"][l], 0, FF), KC, FF),
                    (a["w_sh_down"][l].rearrange("(k p) n -> p k n", p=P), 2, D)]
        straight_a += shared_tiles(0)
        N_A = 2 * NADA + len(straight_a)

        take = carve()
        h_row = take(3, D)
        shT = take(KC, T)
        hs = take(2, T)
        sgs = take(2, T)
        rt = take(12, 3, E)
        g8 = take(3, 8, 8)
        gsx = take(3, 12)
        gs8 = take(3, 8)
        gmk = take(3, 12)
        key8 = take(3, 8)
        w8 = take(3, 8)
        wsum = take(4, 3)
        over = take(P + 8, parts=E)
        cmp = take(E, parts=E)
        code_i = take(3, 8, dt=I32)
        r_i = take(3, 8, dt=I32)
        b_i = take(3, 8, dt=I32)
        place_i = take(3, 8, dt=I32)
        place_f = take(3, 8)
        idx_all = take(NBLK, parts=SLOTS, dt=I32)
        gidx = take(2, parts=SLOTS, dt=I32)
        xg = take(2, D, parts=SLOTS)
        xgT = take(2, KC, SLOTS)
        sg = take(2, 2 * SLOTS)
        hb = take(2, 2 * SLOTS)
        yb = take(2, D, parts=SLOTS)
        yk = take(4, D)
        acc = take(3, D)

        take = carve()
        latc = take(2, PAGES, CL)
        krc = take(2, PAGES, ROPE)
        latcT = take(2, PAGES * P)
        krcT_all = take(PAGES * P)
        krcT = krcT_all[0:ROPE]
        qabs = take(2, AH, T)
        latT = take(2, TPAD)
        krT = take(TPAD, parts=ROPE)
        lat_tok = take(2, CL)
        lat_new = take(CL, parts=TS)
        kr_tok = take(3, ROPE)
        att_work = take(2 * 2 * TP + 2 * 4 * P)
        s2 = att_work[:, 0:4 * TP].rearrange("p (u j k) -> p u j k", u=2, j=2)
        pT = att_work[:, 4 * TP:].rearrange("p (u k) -> p u k", u=2)
        pss = take(17 * AH)
        att = take(80)
        att_row = take(CL, parts=AH)
        ptab = take(TS, dt=I32)
        ptf = take(TS)
        cidx = take(TS, dt=I32)
        hkv = latcT.rearrange("p c n -> p (c n)")[:, 0:KC * T].rearrange("p (c n) -> p c n", c=KC)
        nq = att_work[:, 0:6 * T].rearrange("p (a c n) -> p a c n", a=2, c=3)
        krr = krcT_all[0:ROPE, 3 * T:4 * T]
        qlT = krcT_all[:, 0:3 * T].rearrange("p (c n) -> p c n", c=3)
        wukT = latc[:, 1].rearrange("p t c -> p (t c)")[:, 0:2 * D].rearrange("p (h c) -> p h c", h=AH)
        qnope = hT
        qrope = xn[0:ROPE]

        def straight_b():
            uq = a["w_uq"][0].rearrange("(k p) n -> p k n", p=P)
            t = [(tile_k(a["w_dkv"], 0, 256), KC, 256), (tile_k(a["w_dkv"], 256, 64), KC, 64),
                 (tile_k(a["w_dq"][0], 0, 256), KC, 256), (tile_k(a["w_dq"][0], 256, 128), KC, 128)]
            t += [(uq[:, :, c:min(c + 576, 1536)], 3, min(576, 1536 - c)) for c in range(0, 1536, 576)]
            t += [(a["w_uk"].rearrange("(k p) h n -> p k (h n)", p=P), 2, AH * NOPE),
                  (a["w_uv"].rearrange("(k p) h n -> p k (h n)", p=P), 2, AH * VD)]
            t += [(tile_k(a["w_mla_out"][0], i * 256, 256), KC, 256) for i in range(4)]
            return t + shared_tiles(1)

        tiles_b = straight_b()
        N_B = len(tiles_b)
        sh_at = [N_A - 3, N_B - 3]
        held = [[sum(q % RING == s for q in range(N_A)) for s in range(RING)],
                [sum((N_A + q) % RING == s for q in range(N_B)) for s in range(RING)]]
        before = [N_A, N_B]
        first_slot = [N_A % RING, (N_A + N_B) % RING]

        block = ctx.enter_context(nc.Block())

        @block.sync
        def _(sp):
            w_ada = [a["w_ada"][l].rearrange("(k p) n -> p k n", p=P) for l in range(2)]
            for s in range(RING):
                sp.dma_start(slot(s, KC, 256), w_ada[0][:, :, s * 256:(s + 1) * 256]
                             ).then_inc(ev(f"loadedA{s}"), 16)
            for l in range(2):
                with sp.Fori(1 - l, NADA // RING) as i:
                    for s in range(RING):
                        sp.wait_ge(ev("usedA"), i * RING + (l * NADA - RING + s + 1))
                        sp.dma_start(slot(s, KC, 256), w_ada[l][:, :, bass.ds(i * (RING * 256) + s * 256, 256)]
                                     ).then_inc(ev(f"loadedA{s}"), 16)
            for n, (src, k, cols) in enumerate(straight_a):
                sp.wait_ge(ev("usedA"), 2 * NADA - RING + n + 1)
                sp.dma_start(slot(n % RING, k, cols), src).then_inc(ev(f"loadedA{n % RING}"), 16)

            def experts(l, used_before):
                s0 = first_slot[l]
                gate = a["w_exp_gate"][l].rearrange("e (k p) n -> e p k n", p=P)
                up = a["w_exp_up"][l].rearrange("e (k p) n -> e p k n", p=P)
                down = a["w_exp_down"][l].rearrange("e (k p) n -> e p k n", p=P)

                def block_tiles(u, e, wait):
                    for j, (w, k, n) in enumerate(((gate, KC, FF), (up, KC, FF), (down, 2, D))):
                        s = (s0 + 3 * u + j) % RING
                        wait(3 * u + j)
                        src = w[e] if isinstance(e, int) else w[bass.ds(e, 1)].rearrange("e p k n -> p (e k) n")
                        sp.dma_start(slot(s, k, n), src).then_inc(ev("loaded" + "AB"[l] + str(s)), 16)

                for u in range(2):
                    block_tiles(u, u, used_before)
                used = ev("used" + "AB"[l])
                with sp.Fori(1, E // 2) as i:
                    for u in range(2):
                        block_tiles(u, 2 * i + u, lambda q: sp.wait_ge(used, i * RING + (before[l] + q - RING + 1)))
                sp.wait_ge(ev("table"), 2 * l + 2)
                n = sp.value_load(niter[0:1, l:l + 1], min_val=E // 2 + 1, max_val=(E + MAXOVER) // 2)
                with sp.Fori(E // 2, n) as i:
                    for u in range(2):
                        e = sp.value_load(blk_e[0:1, l, bass.ds(i * 2 + (u - E), 1)], min_val=0, max_val=E - 1)
                        block_tiles(u, e, lambda q: sp.wait_ge(used, i * RING + (before[l] + q - RING + 1)))
                return n

            n0 = experts(0, lambda q: sp.wait_ge(ev("usedA"), N_A - RING + q + 1))

            for q, (src, k, cols) in enumerate(tiles_b):
                if q < RING:
                    sp.wait_ge(ev("usedA"), n0 * RING + (N_A + q - RING + 1))
                else:
                    sp.wait_ge(ev("usedB"), q - RING + 1)
                s = (N_A + q) % RING
                sp.dma_start(slot(s, k, cols), src).then_inc(ev(f"loadedB{s}"), 16)
            experts(1, lambda q: sp.wait_ge(ev("usedB"), N_B - RING + q + 1))
        @block.scalar
        def _(act):
            A = nc.scalar
            chain = Chain(act, ev("act_steps"))

            def load(dst, src, what):
                act.dma_start(dst, src).then_inc(ev(what), 16)

            load(cst[:, :], a["consts"], "in_cst")
            load(c_rows[0:1, :], a["c_prompt"], "in_c")
            load(c_rows[1:9, :], a["c_sample"], "in_c")
            for l in range(2):
                load(rowA[48 * l:48 * l + 48, :], a["b_ada"][l].rearrange("(r n) -> r n", n=P), "in_cols")
            load(rowA[96:112, :], a["b_ada_kv"].rearrange("(r n) -> r n", n=P), "in_cols")
            for l in range(2):
                load(rowB[B_MIX + 8 * l:B_MIX + 8 * l + 8, :], a["g_mix"][l].rearrange("(r n) -> r n", n=P), "in_cols")
                load(rowB[B_FFN + 8 * l:B_FFN + 8 * l + 8, :], a["g_ffn"][l].rearrange("(r n) -> r n", n=P), "in_cols")
            load(rowB[B_KV:B_KV + 8, :], a["g_kv_in"].rearrange("(r n) -> r n", n=P), "in_cols")
            load(rowB[B_FIN:B_FIN + 8, :], a["g_final"].rearrange("(r n) -> r n", n=P), "in_cols")
            load(rowB[B_HEAD:B_HEAD + 8, :], a["g_mlstm_head"][0].rearrange("(r n) -> r n", n=P), "in_cols")
            load(rowB[B_LAT:B_LAT + 2, :], a["g_kv_lat"].rearrange("(r n) -> r n", n=P), "in_cols")
            load(rowB[B_QL:B_QL + 3, :], a["g_q_lat"][0].rearrange("(r n) -> r n", n=P), "in_cols")
            for t in range(2):
                load(x_rows[:, t, :], a["x_prompt"][0, t * P:(t + 1) * P, :], "in_x")
            load(x_rows[0:TS, 2, :], a["x_sample"].rearrange("b s d -> (b s) d"), "in_x")
            for l in range(2):
                load(wrt[:, l], a["w_router"][l].rearrange("(k p) n -> p k n", p=P), "in_router")
                load(brt[:, l], a["b_router"][l:l + 1, :].to_broadcast([P, E]), "in_router")

            act.wait_ge(ev("in_c"), 32)
            A.activation(c_sig[0:9, :], c_rows[0:9, :], ACT.Exp, scale=-1.0).then_inc(ev("c_exp"), 1)

            def norm_root(tag, bank, width, n, reps=1, cols=T):
                act.wait_ge(ev("norm_sum"), NORM[tag])
                for r in range(reps):
                    chain.mark(A.activation(rs[:, r, 0:cols], ps[:, bank + r, 0:cols], ACT.Ln, bias=eps_col,
                                            scale=1.0 / width))
                act.wait_ge(chain.sem, chain.n)
                A.activation(rs[:, 0:reps, 0:cols], rs[:, 0:reps, 0:cols], ACT.Exp, scale=-0.5
                             ).then_inc(ev("norm_rs"), 1)

            act.wait_ge(ev("in_cst"), 16)
            norm_root("mix0", 2, D, 1)

            act.wait_ge(ev("rows_used"), 1)
            with nc.allow_non_contiguous_dma(reason="a few numbers"):
                load(wg, w_in[:, 3072:3080].rearrange("(k p) n -> p k n", p=P), "in_ml")
                load(small[0:H, 0:2], a["b_mlstm_gates"][0].rearrange("(c h) -> h c", h=H), "in_ml")
                load(rowsS[:, 0, :], a["state_mlstm_m"][0].rearrange("b h -> h b"), "in_ml")
            load(nrow[0:H * TS, :], a["state_mlstm_n"][0].rearrange("b h k -> (b h) k"), "in_ml")
            load(c_half, a["state_mlstm_C"][0, 0:4].rearrange("b h k v -> k (b h) v"), "in_c0")

            act.sem_inc(ev("mod_row"), 2)
            for l in range(2):
                if l:
                    act.wait_ge(ev("mod_turned"), l)
                with act.Fori(0, NADA // RING) as i:
                    for s in range(RING):
                        act.wait_ge(ev("usedA"), i * RING + (l * NADA + s + 1))
                        A.activation(mod_rows[:, bass.ds(i * (RING * 256) + s * 256, 256)], ps[0:9, 4 + s % 2, 0:256],
                                     ACT.Copy).then_inc(ev("mod_row"), 1)
            act.wait_ge(ev("mod_turned"), 2)
            for q in range(8):
                act.wait_ge(ev("usedA"), 2 * NADA + q + 1)
                A.activation(mod_rows[:, q * 256:(q + 1) * 256], ps[0:9, 4 + q % 2, 0:256], ACT.Copy
                             ).then_inc(ev("mod_row"), 1)

            act.wait_ge(ev("gate_abs"), 1)
            chain.step(A.activation(gr[:, 2, 0:TP], gr[:, 1, 0:TP], ACT.Exp, scale=-1.0))
            chain.mark(A.activation(rowsS[:, 3, :], rowsS[:, 2, :], ACT.Exp, scale=-1.0))
            chain.step(A.activation(gr[:, 3, 0:TP], gr[:, 2, 0:TP], ACT.Ln, bias=one_col[0:H]))
            A.activation(rowsS[:, 4, :], rowsS[:, 3, :], ACT.Ln, bias=one_col[0:H]).then_inc(ev("gate_ln"), 1)
            for m in range(24):
                act.wait_ge(ev("usedA" if m % 2 else "halfA"), (2 * NADA + 8 if m % 2 else 0) + m // 2 + 1)
                fn, scale = (ACT.Exp, -1.0) if m >= 16 else (ACT.Copy, DK ** -0.5 if 4 <= m < 8 else 1.0)
                A.activation(projT[:, m, :], ps[:, m % 2, 0:T], fn, scale=scale).then_inc(ev("proj_out"), 1)
                if m == 11:
                    act.wait_ge(ev("rows_m"), 1)
                    A.activation(row_wi[:, 0:L], gr[:, 8, L:2 * L], ACT.Exp, bias=small[0:H, 2:3], scale=-1.0
                                 ).then_inc(ev("row_exps"), 1)
                    A.activation(row_wi[:, L:L + 24], rowsS[:, 10:13, :], ACT.Exp).then_inc(ev("row_exps"), 1)

            for h in range(H):
                act.wait_ge(ev("head_vector"), 6 * h + 1)
                A.activation(wmat, wmat, ACT.Exp, scale=-1.0).then_inc(ev("head_scalar"), 1)
                A.activation(enm, ps[:, 0, 2 * L:4 * L], ACT.Exp, scale=-1.0).then_inc(ev("head_scalar"), 1)
                act.wait_ge(ev("head_vector"), 6 * h + 2)
                A.activation(bcs[:, h, :], ps[:, 1, L:L + 24], ACT.Copy).then_inc(ev("head_scalar"), 1)

            norm_root("head", 0, DV, 1, reps=4)
            norm_root("ffn0", 2, D, 1)

            def moe_act(l):
                act.wait_ge(ev("logits"), l + 1)
                A.activation(rt[:, 0].rearrange("p t e -> p (t e)"), ps[:, 0, 0:3 * E], ACT.Exp, scale=-1.0
                             ).then_inc(ev("sig_exp"), 1)
                for t in range(3):
                    n = P if t < 2 else TS
                    act.wait_ge(ev("h_row_ps"), 3 * l + t + 1)
                    chain.step(A.activation(h_row[0:n, t, :], ps[0:n, 1 + 2 * t:3 + 2 * t, :].rearrange("p a n -> p (a n)"),
                                            ACT.Copy))
                    act.dma_start(h_rows[t * P:t * P + n, :], h_row[0:n, t, :]).then_inc(ev("h_stored"), 16)
                for j in range(2):
                    if j == 0:
                        act.wait_ge(ev("used" + "AB"[l]), sh_at[l] + 1)
                    A.activation(sgs[:, j, :], ps[:, 3 + j, 0:T], ACT.Silu).then_inc(ev("sh_silu"), 1)
                act.wait_ge(ev("table"), 2 * l + 2)
                n = act.value_load(niter[0:1, l:l + 1], min_val=E // 2 + 1, max_val=(E + MAXOVER) // 2)
                used = ev("used" + "AB"[l])
                act.wait_ge(ev("y_zero"), 32)
                act.sem_inc(ev(f"y_stored{l}_0"), 16)
                act.sem_inc(ev(f"y_stored{l}_1"), 16)
                act.sem_inc(ev(f"y_out{l}"), 2)
                with act.Fori(0, n) as i:
                    for u in range(2):
                        act.wait_ge(used, i * 6 + (before[l] + 3 * u + 2))
                        A.activation(sg[:, u, :], ps[:, 1 + u, 0:2 * SLOTS], ACT.Silu).then_inc(ev(f"silu{l}"), 1)
                        act.wait_ge(used, i * 6 + (before[l] + 3 * u + 3))
                        act.wait_ge(ev(f"y_stored{l}_{u}"), i * 16 + 16)
                        A.activation(yb[:, u, :], ps[0:SLOTS, 3 + 2 * u:5 + 2 * u, :].rearrange("p a n -> p (a n)"),
                                     ACT.Copy).then_inc(ev(f"y_out{l}"), 1)
                        act.wait_ge(ev(f"y_out{l}"), i * 2 + (u + 3))
                        act.dma_start(y_slots[bass.ds(i * (2 * SLOTS) + u * SLOTS, SLOTS), :], yb[:, u, :]
                                      ).then_inc(ev(f"y_stored{l}_{u}"), 16)

            moe_act(0)

            norm_root("mix1", 2, D, 1)
            norm_root("lat", 3, CL, 1)
            act.wait_ge(ev("lat_tok_ps"), 1)
            A.activation(lat_tok.rearrange("p t c -> p (t c)"), ps[:, 5, :], ACT.Copy).then_inc(ev("lat_tok"), 1)
            A.activation(lat_new, ps[0:TS, 6, 0:CL], ACT.Copy).then_inc(ev("lat_tok"), 1)
            A.activation(kr_tok[:, 0:2, :].rearrange("p t c -> p (t c)"), ps[:, 7, 0:2 * ROPE], ACT.Copy).then_inc(ev("lat_tok"), 1)
            A.activation(kr_tok[0:TS, 2, :], ps[0:TS, 7, 2 * ROPE:3 * ROPE], ACT.Copy).then_inc(ev("lat_tok"), 1)
            norm_root("ql", 3, QL, 1)
            for h in range(AH):
                act.wait_ge(ev("q_nope_ps"), h + 1)
                A.activation(qnope[:, h, 0:T], ps[:, h % 2, 0:T], ACT.Copy).then_inc(ev("q_nope"), 1)
            for g in range(4):
                if g < 3:
                    act.wait_ge(ev("wukT_ps"), g + 1)
                else:
                    act.wait_ge(ev("usedB"), 8)
                A.activation(wukT[:, 2 * g:2 * g + 2, :].rearrange("p h c -> p (h c)"), ps[:, 4 + g, :], ACT.Copy
                             ).then_inc(ev("wukT"), 1)
            for m in range(2 * AH):
                act.wait_ge(ev("q_abs_ps"), m + 1)
                A.activation(qabs[:, m % 2, m // 2, :], ps[:, m % 4, 0:T], ACT.Copy).then_inc(ev("q_abs"), 1)

            for n in range(8):
                nk = P * (n // 4 + 1)
                act.wait_ge(ev("unit_vector"), 4 * n + 2)
                for j in range(2):
                    A.activation(s2[:, n % 2, j, 0:nk], s2[:, n % 2, j, 0:nk], ACT.Exp, bias=att[:, 4 * (n % 2) + j:4 * (n % 2) + j + 1],
                                 accum_out=att[:, 4 * (n % 2) + 2 + j:4 * (n % 2) + 3 + j]).then_inc(ev("unit_scalar"), 1)
                act.wait_ge(ev("p_turned"), n + 1)
                if n < 4:
                    A.activation(pT[:, n % 2].rearrange("p (j k) -> p j k", j=2)[:, :, 0:P],
                                 ps[:, 2 + n % 2, :].rearrange("p (j k) -> p j k", j=2)[:, :, 0:P], ACT.Copy
                                 ).then_inc(ev("unit_scalar"), 1)
                else:
                    A.activation(pT[:, n % 2], ps[:, 2 + n % 2, :], ACT.Copy).then_inc(ev("unit_scalar"), 1)

            act.sem_inc(ev("c_out_a"), 2)

            def cache_out(b, g):
                act.wait_ge(ev("c_turned"), b * 12 + (g + 1))
                dst = latcT[:, g // 4, (g % 4) * 512:(g % 4 + 1) * 512] if g < 8 else krcT[:, (g - 8) * 512:(g - 7) * 512]
                src = ps[:, g % 4, :] if g < 8 else ps[0:ROPE, g % 4, :]
                A.activation(dst, src, ACT.Copy).then_inc(ev("c_out_a"), 1)

            def seq_act(b, more):
                for g in (1, 3, 5, 7) if more else ():
                    cache_out(b + 1, g)
                act.wait_ge(ev("seq_vector"), b * 5 + 3)
                A.activation(pss, pss, ACT.Exp).then_inc(ev("s_exp"), 1)
                for g in (9, 11) if more else ():
                    cache_out(b + 1, g)

            for g in range(1, 12, 2):
                cache_out(0, g)
            with act.Fori(0, 3) as i:
                for u in range(2):
                    seq_act(i * 2 + u, True)
            seq_act(6, True)
            seq_act(7, False)
            for h in range(AH):
                if h < AH - 1:
                    act.wait_ge(ev("o_ps"), h + 1)
                else:
                    act.wait_ge(ev("usedB"), 9)
                A.activation(hT[:, h, 0:T], ps[:, h % 2, 0:T], ACT.Copy).then_inc(ev("o_T"), 1)
            norm_root("ffn1", 2, D, 1)
            moe_act(1)
            norm_root("fin", 2, D, 1)
            for t in range(3):
                n_t = P if t < 2 else TS
                act.wait_ge(ev("y_ps"), t + 1)
                A.activation(h_row[0:n_t, t, :], ps[0:n_t, 3 + 2 * (t % 2):5 + 2 * (t % 2), :].rearrange("p a n -> p (a n)"),
                             ACT.Copy).then_inc(ev("y_row"), 1)
                act.wait_ge(ev("y_row"), t + 1)
                dst = y_p[0, t * P:(t + 1) * P, :] if t < 2 else y_s.rearrange("b s d -> (b s) d")
                act.dma_start(dst, h_row[0:n_t, t, :]).then_inc(ev("y_done"), 16)
            act.wait_ge(ev("y_done"), 48)
        @block.tensor
        def _(pe):
            def mm(out, lhsT, rhs, start=True, stop=True):
                return nc.tensor.matmul(out, lhsT, rhs, start=start, stop=stop)

            def tr(out, in_, parts=P):
                return nc.tensor.matmul(out, in_, ident[0:parts, 0:parts], start=True, stop=True,
                                        is_transpose=True)

            pe.wait_ge(ev("in_cst"), 16)
            pe.wait_ge(ev("in_cols"), 12 * 16)
            tr(ps[:, 1, 0:112], rowA[0:112, :], 112)
            tr(ps[:, 1, 112:173], rowB[0:61, :], 61).then_inc(ev("turned"), 1)
            pe.wait_ge(ev("cs_rows"), 1)
            for c in range(KC):
                ins = tr(ps[:, 0, 9 * c:9 * c + 9], c_sig[0:9, c * P:(c + 1) * P], 9)
            ins.then_inc(ev("turned"), 1)
            pe.wait_ge(ev("in_x"), 48)
            for t in range(2):
                for c in range(KC):
                    ins = tr(ps[:, 2 + 2 * t + c // 4, (c % 4) * P:(c % 4 + 1) * P], x_rows[:, t, c * P:(c + 1) * P])
            for c in range(KC):
                ins = tr(ps[:, 6, 8 * c:8 * c + 8], x_rows[0:TS, 2, c * P:(c + 1) * P], TS)
            ins.then_inc(ev("turned"), 1)

            def norm_sum(tag, bank, src, groups=1):
                pe.wait_ge(ev("norm_sq"), NORM[tag])
                n = KC // groups
                for g in range(groups):
                    for c in range(n):
                        ins = mm(ps[:, bank + g, 0:T], ones, src[:, g * n + c, 0:T], c == 0, c == n - 1)
                ins.then_inc(ev("norm_sum"), 1)

            pe.wait_ge(ev("cols_out"), 8)
            norm_sum("mix0", 2, xn)

            def ada_product(w, bank):
                for k in range(KC):
                    ins = mm(ps[0:9, bank, 0:256], csT[:, k, :], w[:, k, :], k == 0, k == KC - 1)
                ins.then_inc(ev("usedA"), 1)

            def turn_mod(l, bank, chunks):
                pe.wait_ge(ev("mod_row"), 2 + NADA * l + chunks // 2)
                for m in range(chunks):
                    ins = tr(ps[:, bank, 9 * m:9 * m + 9], mod_rows[:, m * P:(m + 1) * P], 9)
                ins.then_inc(ev("mod_turned"), 1)

            for l in range(2):
                with pe.Fori(0, NADA // RING) as i:
                    for s in range(RING):
                        pe.wait_ge(ev("mod_row"), i * RING + (l * NADA + s + 1))
                        pe.wait_ge(ev(f"loadedA{s}"), i * 16 + (16 + l * 16 * (NADA // RING)))
                        ada_product(slot(s, KC, 256), 4 + s % 2)
                turn_mod(l, 6 + l, 48)
            at = [0]

            def next_tile(k, n):
                q = at[0]
                at[0] += 1
                if q < len(straight_a):
                    pe.wait_ge(ev(f"loadedA{q % RING}"), 16 * (2 * NADA // RING + q // RING + 1))
                    return slot(q % RING, k, n)
                q -= N_A - 2 * NADA
                s = (N_A + q) % RING
                pe.wait_ge(ev(f"loadedB{s}"), 16 * (q // RING + 1))
                return slot(s, k, n)

            for q in range(8):
                pe.wait_ge(ev("mod_row"), 2 * NADA + q + 1)
                ada_product(next_tile(KC, 256), 4 + q % 2)
            turn_mod(2, 0, 16)

            def projections(ph, tiles, rhs, free):
                m = 0
                for q in range(tiles):
                    w = next_tile(KC, 256)
                    for j in range(2):
                        if m >= 2:
                            pe.wait_ge(ev(free), m - 1)
                        for k in range(KC):
                            ins = mm(ps[:, m % 2, 0:T], w[:, k, j * P:(j + 1) * P], rhs[:, k, 0:T],
                                     k == 0, k == KC - 1)
                        ins.then_inc(ev(("used" if j else "half") + ph), 1)
                        m += 1

            pe.wait_ge(ev("modkv"), 1)
            pe.wait_ge(ev("h_ready"), H_READY["mix0"])
            pe.wait_ge(ev("in_ml"), 64)
            for g in range(2):
                for k in range(KC):
                    ins = mm(ps[0:H, 4 + g, 0:T], wg[:, k, 4 * g:4 * g + 4], hT[:, k, 0:T], k == 0, k == KC - 1)
            ins.then_inc(ev("gates"), 1)
            tr(ps[:, 2, 300:332], nrow[0:H * TS, :], H * TS).then_inc(ev("nT_ps"), 1)
            projections("A", 12, hT, "proj_out")

            pe.wait_ge(ev("proj_out"), 24)
            pe.wait_ge(ev("rows_u"), 1)
            for t in range(2):
                ins = tr(ps[:, 3, 4 * t:4 * t + 4], gr[:, 5, t * L:(t + 1) * L], H)
            ins.then_inc(ev("u_ps"), 1)
            for g in range(6):
                if g >= 4:
                    pe.wait_ge(ev("kv_tok"), g - 3)
                t, c0 = (g, 4) if g < 2 else ((g - 2) // 2, 8 + 4 * (g % 2))
                for c in range(4):
                    ins = tr(ps[:, 4 + g % 4, c * P:(c + 1) * P], projT[:, c0 + c, t * L:(t + 1) * L])
                ins.then_inc(ev("kv_tok_ps"), 1)

            for h in range(H):
                if h:
                    pe.wait_ge(ev("head_vector"), 6 * h - 4)
                    pe.wait_ge(ev("head_scalar"), 3 * h - 1)
                    pe.wait_ge(ev("head_scalar"), 3 * h)
                else:
                    pe.wait_ge(ev("row_exps"), 2)
                sel = cst[0:H, C_SEL + h * P:C_SEL + (h + 1) * P]
                mm(ps[:, 0, 0:4 * L], sel, gr[:, 8:10, :])
                mm(ps[:, 1, 0:L + 24], sel, row_wi)
                for t in range(2):
                    ins = mm(ps[:, 2, t * L:(t + 1) * L], projT[:, 4 + h, t * L:(t + 1) * L],
                             projT[:, h, t * L:(t + 1) * L])
                ins.then_inc(ev("head_tensor"), 1)
                pe.wait_ge(ev("head_vector"), 6 * h + 3)
                if not h:
                    pe.wait_ge(ev("kv_tok"), 6)
                for t in range(2):
                    ins = mm(ps[:, 3 + t, 0:VA], ka[:, t, :], v_tok[:, t, h, :])
                ins.then_inc(ev("head_tensor"), 1)
                pe.wait_ge(ev("head_vector"), 6 * h + 4)
                for t in range(2):
                    for j in range(2):
                        o = ps[:, 5, (2 * j + t) * L:(2 * j + t + 1) * L]
                        mm(o, v_tok[:, t, h, j * P:(j + 1) * P], smat[:, t, :], True, t == 0)
                        if t:
                            mm(o, c1[:, j * P:(j + 1) * P], qw, False, True)
                    o = ps[:, 6, t * L:(t + 1) * L]
                    ins = mm(o, ones, smat[:, t, :], True, t == 0)
                    if t:
                        ins = mm(o, nb, qw, False, True)
                ins.then_inc(ev("head_tensor"), 1)

            pe.wait_ge(ev("seq_prod"), 1)
            mm(ps[:, 7, 0:2 * H * TS], ones, smp[:, 0:2, :]).then_inc(ev("seq_ps"), 1)
            pe.wait_ge(ev("seq_prod"), 2)
            pe.wait_ge(ev("head_vector"), 6 * H)
            for h in range(H):
                tr(ps[0:TS, 0, h * P:(h + 1) * P], smp[:, 2, h * TS:(h + 1) * TS])
            for c in range(8):
                ins = tr(ps[0:TS, 1 + c // 4, (c % 4) * P:(c % 4 + 1) * P], projT[:, 8 + c, TP:T])
            ins.then_inc(ev("seq_ps"), 1)
            n = 0
            for b in range(TS):
                if b % 4 == 0:
                    pe.wait_ge(ev(f"in_c{b // 4}"), 16)
                for h in range(H):
                    for j in range(2):
                        ins = mm(ps[:, 7, 64 + (h * 2 + j) * TS + b:64 + (h * 2 + j) * TS + b + 1],
                                 c_half[:, (b % 4) * H + h, j * P:(j + 1) * P], projT[:, h, TP + b:TP + b + 1])
                ins.then_inc(ev("s_qc"), 1)
                pe.wait_ge(ev("s_kone"), b + 1)
                for h in range(H):
                    if n >= 2:
                        pe.wait_ge(ev("s_cnew"), n - 1)
                    mm(ps[:, 3 + n % 2, 0:DV], k_one[:, h * P:(h + 1) * P], v_row[:, h * DV:(h + 1) * DV]
                       ).then_inc(ev("s_outer"), 1)
                    n += 1
            pe.wait_ge(ev("seq_prod"), 3)
            tr(ps[0:H * TS, 5, 0:P], smp[:, 4, :]).then_inc(ev("seq_ps"), 1)
            pe.wait_ge(ev("head_vector"), 6 * H - 1)
            tr(ps[0:H, 6, 0:P], small[:, 16:20]).then_inc(ev("seq_ps"), 1)

            norm_sum("head", 0, xn, H)

            pe.wait_ge(ev("mix_h"), 1)
            projections("A", 4, hh, "x_out")
            norm_sum("ffn0", 2, xn)

            def moe_pe(l, ph):
                pe.wait_ge(ev("h_ready"), H_READY[f"ffn{l}"])
                pe.wait_ge(ev("in_router"), 64)
                for t in range(3):
                    for k in range(KC):
                        ins = mm(ps[:, 0, t * E:(t + 1) * E], hT[:, k, t * P:(t + 1) * P], wrt[:, l, k, :],
                                 k == 0, k == KC - 1)
                ins.then_inc(ev("logits"), 1)
                for t in range(3):
                    n = P if t < 2 else TS
                    for c in range(KC):
                        ins = tr(ps[0:n, 1 + 2 * t + c // 4, (c % 4) * P:(c % 4 + 1) * P], hT[:, c, t * P:t * P + n])
                    ins.then_inc(ev("h_row_ps"), 1)
                pe.wait_ge(ev("h_stored"), 48 * l + 48)
                for g in range(2):
                    w = next_tile(KC, FF)
                    for j in range(2):
                        for k in range(KC):
                            ins = mm(ps[:, 3 + 2 * g + j, 0:T], w[:, k, j * P:(j + 1) * P], hT[:, k, 0:T],
                                     k == 0, k == KC - 1)
                    ins.then_inc(ev("used" + ph), 1)
                pe.wait_ge(ev("mask"), 3 * l + 3)
                mask = rt[:, 7]
                striu = cst[:, C_STRIU:C_STRIU + P]
                for t in range(3):
                    for s in range(t + 1):
                        mm(ps[:, 0, (3 + t) * E:(4 + t) * E], striu if s == t else ones, mask[:, s, :], s == 0, s == t)
                for t in range(3):
                    ins = mm(ps[0:E, 7, 0:1], mask[:, t, :], ones[:, 0:1], t == 0, t == 2)
                ins.then_inc(ev("route_ps"), 1)
                pe.wait_ge(ev("route_in"), 2 * l + 1)
                mm(ps[:, 7, 72:72 + E], over[:, 0:P], striu[0:E, 0:E])
                mm(ps[0:E, 7, 136:137], cst[0:E, C_TRIU:C_TRIU + E], over[:, 0:1])
                mm(ps[0:1, 7, 137:138], over[:, 0:1], ones[0:E, 0:1]).then_inc(ev("route_ps"), 1)
                pe.wait_ge(ev("route_in"), 2 * l + 2)
                mm(ps[0:1, 3, 0:E], ones[0:E, 0:1], cmp).then_inc(ev("route_ps"), 1)
                pe.wait_ge(ev("sh_hidden"), l + 1)
                w = next_tile(2, D)
                for m in range(KC):
                    if m >= 2:
                        pe.wait_ge(ev("sh_out"), 8 * l + m - 1)
                    for k in range(2):
                        ins = mm(ps[:, 1 + m % 2, 0:T], w[:, k, m * P:(m + 1) * P], hs[:, k, :], k == 0, k == 1)
                    ins.then_inc(ev("sh_down" if m < KC - 1 else "used" + ph), 1)

                n = pe.value_load(niter[0:1, l:l + 1], min_val=E // 2 + 1, max_val=(E + MAXOVER) // 2)
                pe.wait_ge(ev("sh_out"), 8 * l + KC)
                s0, used = first_slot[l], ev("used" + ph)
                pe.sem_inc(ev(f"xgT_ps{l}"), 1)

                def turn(u):
                    for c in range(KC):
                        ins = tr(ps[:, 0, c * SLOTS:(c + 1) * SLOTS], xg[:, u, c * P:(c + 1) * P], SLOTS)
                    ins.then_inc(ev(f"xgT_ps{l}"), 1)

                pe.wait_ge(ev(f"gath{l}_0"), 16)
                pe.wait_ge(ev(f"xgT{l}"), 1)
                turn(0)
                with pe.Fori(0, n) as i:
                    for u in range(2):
                        pe.wait_ge(ev(f"xgT{l}"), i * 2 + (u + 2))
                        pe.wait_ge(ev(f"hb{l}"), i * 2 + (u + 1))
                        for g in range(2):
                            s = (s0 + 3 * u + g) % RING
                            pe.wait_ge(ev("loaded" + ph + str(s)), i * 16 + 16 * (held[l][s] + 1))
                            w = slot(s, KC, FF)
                            for j in range(2):
                                for k in range(KC):
                                    c = (2 * g + j) * SLOTS
                                    ins = mm(ps[:, 1 + u, c:c + SLOTS], w[:, k, j * P:(j + 1) * P], xgT[:, u, k, :],
                                             k == 0, k == KC - 1)
                            ins.then_inc(used, 1)
                        pe.wait_ge(ev(f"gath{l}_{1 - u}"), i * 16 + 16 * (u + 1))
                        nc.tensor.nop(nofuse=True)
                        turn(1 - u)
                        pe.wait_ge(ev(f"hb{l}"), i * 2 + (u + 3))
                        pe.wait_ge(ev(f"y_out{l}"), i * 2 + (u + 1))
                        s = (s0 + 3 * u + 2) % RING
                        pe.wait_ge(ev("loaded" + ph + str(s)), i * 16 + 16 * (held[l][s] + 1))
                        w = slot(s, 2, D)
                        for half in range(2):
                            for k in range(2):
                                ins = mm(ps[0:SLOTS, 3 + 2 * u + half, :], hb[:, u, k * SLOTS:(k + 1) * SLOTS],
                                         w[:, k, half * 512:(half + 1) * 512], k == 0, k == 1)
                        ins.then_inc(used, 1)
                for t in range(3):
                    n_t = P if t < 2 else TS
                    pe.wait_ge(ev("acc"), 24 * l + 8 * (t + 1))
                    for c in range(KC):
                        if t < 2:
                            o = ps[:, 2 * t + c // 4, (c % 4) * P:(c % 4 + 1) * P]
                        else:
                            o = ps[:, 4, c * TS:(c + 1) * TS]
                        ins = tr(o, acc[0:n_t, t, c * P:(c + 1) * P], n_t)
                    ins.then_inc(ev("accT"), 1)

            moe_pe(0, "A")

            norm_sum("mix1", 2, xn)
            pe.wait_ge(ev("h_ready"), H_READY["kv"])
            w = next_tile(KC, 256)
            for j in range(2):
                for k in range(KC):
                    ins = mm(ps[:, j, 0:T], w[:, k, j * P:(j + 1) * P], hkv[:, k, :], k == 0, k == KC - 1)
            ins.then_inc(ev("usedB"), 1)
            w = next_tile(KC, ROPE)
            for k in range(KC):
                ins = mm(ps[0:ROPE, 4, 0:T], w[:, k, :], hkv[:, k, :], k == 0, k == KC - 1)
            ins.then_inc(ev("usedB"), 1)

            def sum_chunks(tag, bank, src, n):
                pe.wait_ge(ev("norm_sq"), NORM[tag])
                for c in range(n):
                    ins = mm(ps[:, bank, 0:T], ones, src[:, c, :], c == 0, c == n - 1)
                ins.then_inc(ev("norm_sum"), 1)

            rot = cst[0:ROPE, C_ROT:C_ROT + ROPE]
            sum_chunks("lat", 3, nq[:, 1], 2)
            pe.wait_ge(ev("kr_raw"), 1)
            mm(ps[0:ROPE, 4, 0:T], rot, krr).then_inc(ev("kr_rot"), 1)
            pe.wait_ge(ev("h_ready"), H_READY["mix1"])
            m = 0
            for q in range(2):
                w = next_tile(KC, 256 - P * q)
                for j in range(2 - q):
                    for k in range(KC):
                        ins = mm(ps[:, m, 0:T], w[:, k, j * P:(j + 1) * P], hT[:, k, 0:T], k == 0, k == KC - 1)
                    m += 1
                ins.then_inc(ev("usedB"), 1)
            pe.wait_ge(ev("lat_T"), 1)
            pe.wait_ge(ev("kr_T"), 1)
            for t in range(2):
                for c in range(2):
                    tr(ps[:, 5, (2 * t + c) * P:(2 * t + c + 1) * P], latT[:, c, t * P:(t + 1) * P])
                tr(ps[:, 7, t * ROPE:(t + 1) * ROPE], krT[:, t * P:(t + 1) * P], ROPE)
            for c in range(2):
                tr(ps[0:TS, 6, c * P:(c + 1) * P], latT[:, c, TP:T])
            tr(ps[0:TS, 7, 2 * ROPE:3 * ROPE], krT[:, TP:T], ROPE).then_inc(ev("lat_tok_ps"), 1)
            sum_chunks("ql", 3, nq[:, 1], 3)
            pe.wait_ge(ev("ql_T"), 1)
            for h in range(AH):
                if h % 3 == 0:
                    w = next_tile(3, 576 if h < 6 else 384)
                c0 = (h % 3) * (NOPE + ROPE)
                if h >= 2:
                    pe.wait_ge(ev("q_nope"), h - 1)
                for k in range(3):
                    ins = mm(ps[:, h % 2, 0:T], w[:, k, c0:c0 + NOPE], qlT[:, k, :], k == 0, k == 2)
                ins.then_inc(ev("q_nope_ps"), 1)
                if h >= 2:
                    pe.wait_ge(ev("q_rope_raw"), h - 1)
                for k in range(3):
                    ins = mm(ps[0:ROPE, 2 + h % 2, 0:T], w[:, k, c0 + NOPE:c0 + NOPE + ROPE], qlT[:, k, :], k == 0, k == 2)
                ins.then_inc(ev("usedB" if h % 3 == 2 or h == AH - 1 else "q_rope_ps"), 1)
            w = next_tile(2, AH * NOPE)
            pe.wait_ge(ev("lat_tok"), 4)
            for g in range(4):
                for j in range(4):
                    h, c = 2 * g + j // 2, j % 2
                    ins = tr(ps[:, 4 + g, j * P:(j + 1) * P], w[:, c, h * NOPE:(h + 1) * NOPE])
                ins.then_inc(ev("wukT_ps" if g < 3 else "usedB"), 1)
            for m in range(2 * AH):
                if m % 4 == 0:
                    pe.wait_ge(ev("wukT"), m // 4 + 1)
                if m == 0:
                    pe.wait_ge(ev("q_nope"), AH)
                    pe.wait_ge(ev("q_rope_raw"), AH)
                if m >= 4:
                    pe.wait_ge(ev("q_abs"), m - 3)
                h, c = m // 2, m % 2
                mm(ps[:, m % 4, 0:T], wukT[:, h, c * P:(c + 1) * P], qnope[:, h, 0:T]).then_inc(ev("q_abs_ps"), 1)
            for h in range(AH):
                if h >= 4:
                    pe.wait_ge(ev("q_rot_out"), h - 3)
                if h == 0:
                    pe.wait_ge(ev("wukT"), 4)
                mm(ps[0:ROPE, 4 + h % 4, 0:T], rot, qrope[:, h, :]).then_inc(ev("q_rot"), 1)

            pe.wait_ge(ev("q_abs"), 2 * AH)
            pe.wait_ge(ev("q_rope"), 1)

            def scores(n):
                t, nk = n // 4, P * (n // 4 + 1)
                if n >= 2:
                    pe.wait_ge(ev("unit_vector"), 4 * n - 7)
                for j in range(2):
                    h = 2 * (n % 4) + j
                    o = ps[:, n % 2, j * TP:j * TP + nk]
                    for c in range(2):
                        mm(o, qabs[:, c, h, t * P:(t + 1) * P], latT[:, c, 0:nk], c == 0, False)
                    ins = mm(o, qrope[:, h, t * P:(t + 1) * P], krT[:, 0:nk], False, True)
                ins.then_inc(ev("p_scores"), 1)

            scores(0)
            for n in range(8):
                t = n // 4
                if n < 7:
                    scores(n + 1)
                pe.wait_ge(ev("unit_vector"), 4 * n + 3)
                if n >= 2:
                    pe.wait_ge(ev("unit_scalar"), 3 * n - 3)
                for j in range(2):
                    for k in range(t + 1):
                        ins = tr(ps[:, 2 + n % 2, (2 * j + k) * P:(2 * j + k + 1) * P], s2[:, n % 2, j, k * P:(k + 1) * P])
                ins.then_inc(ev("p_turned"), 1)
                pe.wait_ge(ev("unit_scalar"), 3 * n + 3)
                if n >= 2:
                    pe.wait_ge(ev("unit_vector"), 4 * n - 4)
                for c in range(2):
                    for j in range(2):
                        for k in range(t + 1):
                            ins = mm(ps[:, 4 + n % 2, (2 * c + j) * P:(2 * c + j + 1) * P], lat_tok[:, k, c * P:(c + 1) * P],
                                     pT[:, n % 2, (2 * j + k) * P:(2 * j + k + 1) * P], k == 0, k == t)
                ins.then_inc(ev("p_olat_ps"), 1)

            def turn_cache(b, u, groups):
                for g in groups:
                    pe.wait_ge(ev("c_out_d" if g % 2 == 0 else "c_out_a"), b * 6 + (g // 2 + 1))
                    nc.tensor.nop(nofuse=True)
                    for j in range(4):
                        t = 4 * (g % 4) + j
                        if g < 8:
                            ins = tr(ps[:, g % 4, j * P:(j + 1) * P], latc[:, u, t, (g // 4) * P:(g // 4 + 1) * P])
                        else:
                            ins = tr(ps[0:ROPE, g % 4, j * P:(j + 1) * P], krc[:, u, t, :])
                    ins.then_inc(ev("c_turned"), 1)

            def seq_pe(b, i, u, more):
                pe.wait_ge(ev("c_out_d"), b * 6 + 8)
                pe.wait_ge(ev("c_out_a"), b * 6 + 8)
                tok = bass.ds(b + TP, 1) if not isinstance(b, int) else slice(b + TP, b + TP + 1)
                for t in range(PAGES + 1):
                    o = ps[:, 4, t * AH:(t + 1) * AH]
                    for c in range(2):
                        lhsT = latcT[:, c, t * P:(t + 1) * P] if t < PAGES else latT[:, c, TP:TPAD]
                        mm(o, lhsT, qabs[:, c, :, tok], c == 0, False)
                    lhsT = krcT[:, t * P:(t + 1) * P] if t < PAGES else krT[:, TP:TPAD]
                    ins = mm(o, lhsT, qrope[:, :, tok], False, True)
                ins.then_inc(ev("seq_tensor"), 1)
                if more:
                    pe.wait_ge(ev(f"cache{1 - u}"), i * 32 + 32 * (u + 1))
                    turn_cache(b + 1, 1 - u, range(4))
                pe.wait_ge(ev("seq_vector"), b * 5 + 1)
                nc.tensor.nop(nofuse=True)
                tr(ps[0:AH, 5, 0:P], att[:, 0:AH]).then_inc(ev("seq_tensor"), 1)
                if more:
                    turn_cache(b + 1, 1 - u, range(4, 8))
                pe.wait_ge(ev("seq_vector"), b * 5 + 2)
                mm(ps[:, 5, 128:136], ones[0:AH, :], att[0:AH, 8:16]).then_inc(ev("seq_tensor"), 1)
                if more:
                    turn_cache(b + 1, 1 - u, range(8, 12))
                pe.wait_ge(ev("s_exp"), b + 1)
                for t in range(PAGES + 1):
                    values, m = (latc[:, u, t, :], P) if t < PAGES else (lat_new, TS)
                    ins = mm(ps[0:AH, 6, 0:CL], pss[0:m, t * AH:(t + 1) * AH], values, t == 0, t == PAGES)
                ins.then_inc(ev("seq_tensor"), 1)
                pe.wait_ge(ev("seq_vector"), b * 5 + 4)
                mm(ps[:, 5, 136:144], ones, att[:, 16:24])
                pe.wait_ge(ev("att_row"), b + 1)
                nc.tensor.nop(nofuse=True)
                for c in range(2):
                    ins = tr(ps[:, 6, CL + c * AH:CL + (c + 1) * AH], att_row[:, c * P:(c + 1) * P], AH)
                ins.then_inc(ev("seq_tensor"), 1)

            pe.wait_ge(ev("cache0"), 32)
            turn_cache(0, 0, range(12))
            with pe.Fori(0, 3) as i:
                for u in range(2):
                    seq_pe(i * 2 + u, i, u, True)
            seq_pe(6, 3, 0, True)
            seq_pe(7, 3, 1, False)

            w = next_tile(2, AH * VD)
            pe.wait_ge(ev("seq_vector"), 5 * TS)
            for h in range(AH):
                if h >= 2:
                    pe.wait_ge(ev("o_T"), h - 1)
                for c in range(2):
                    ins = mm(ps[:, h % 2, 0:T], w[:, c, h * VD:(h + 1) * VD], qabs[:, c, h, :], c == 0, c == 1)
                ins.then_inc(ev("o_ps" if h < AH - 1 else "usedB"), 1)
            pe.wait_ge(ev("o_T"), AH)
            projections("B", 4, hT, "x1_out")
            norm_sum("ffn1", 2, xn)
            moe_pe(1, "B")
            norm_sum("fin", 2, xn)
            pe.wait_ge(ev("y_T"), 1)
            for t in range(3):
                n = P if t < 2 else TS
                if t == 2:
                    pe.wait_ge(ev("y_row"), 1)
                for c in range(KC):
                    ins = tr(ps[0:n, 3 + 2 * (t % 2) + c // 4, (c % 4) * P:(c % 4 + 1) * P], xn[:, c, t * P:t * P + n])
                ins.then_inc(ev("y_ps"), 1)
        @block.vector
        def _(dve):
            V = nc.vector
            ch = Chain(dve, ev("dve_steps"))
            step = ch.step

            dve.wait_ge(ev("c_exp"), 1)
            step(V.tensor_scalar(c_sig[0:9, :], c_sig[0:9, :], 1.0, None, ALU.add))
            step(V.reciprocal(c_sig[0:9, :], c_sig[0:9, :]))
            V.tensor_tensor(c_sig[0:9, :], c_sig[0:9, :], c_rows[0:9, :], ALU.mult).then_inc(ev("cs_rows"), 1)
            dve.wait_ge(ev("turned"), 1)
            V.tensor_copy(colA[:, :], ps[:, 1, 0:112]).then_inc(ev("cols_out"), 1)
            V.tensor_copy(colB[:, :], ps[:, 1, 112:173]).then_inc(ev("cols_out"), 1)
            dve.wait_ge(ev("turned"), 2)
            V.tensor_copy(csT[:, :, :], ps[:, 0, 0:72].rearrange("p (c n) -> p c n", n=9)).then_inc(ev("cols_out"), 1)
            dve.wait_ge(ev("turned"), 3)
            for t in range(2):
                for g in range(2):
                    V.tensor_copy(xT[:, 4 * g:4 * g + 4, t * P:(t + 1) * P],
                                  ps[:, 2 + 2 * t + g, :].rearrange("p (c n) -> p c n", n=P)
                                  ).then_inc(ev("cols_out"), 1)
            V.tensor_copy(xT[:, :, TP:T], ps[:, 6, 0:64].rearrange("p (c n) -> p c n", n=TS)).then_inc(ev("cols_out"), 1)
            step(V.tensor_copy(tok_i[:, :], cst[:, C_TOK:C_TOK + 3]))
            ch.mark(V.memset(zero_row[:, :], 0.0))
            dve.memset(zero_i[:, :], 0).then_inc(ev("zeros"), 1)
            dve.wait_ge(ev("cols_out"), 8)

            def square(tag, dst, src):
                V.tensor_tensor(dst, src, src, ALU.mult).then_inc(ev("norm_sq"), 1)

            def normalise(tag):
                dve.wait_ge(ev("norm_rs"), NORM[tag])
                step(V.tensor_tensor(xn[:, :, :], xT[:, :, :], rep(rs[:, 0, :], 1, KC), ALU.mult))

            def modulate(tag, dst, gain, shift, scale):
                step(V.scalar_tensor_tensor(out=amod[:, :, :], in0=modT[:, scale:scale + KC, :], scalar=1.0,
                                            in1=rep(colB[:, gain:gain + KC], 2, 9), op0=ALU.add, op1=ALU.mult))
                for c in range(KC):
                    ch.mark(V.tensor_scalar(dst[:, c, 0:TP], xn[:, c, 0:TP], amod[:, c, 0:1],
                                            modT[:, shift + c, 0:1], ALU.mult, ALU.add))
                step(V.tensor_tensor(dst[:, :, TP:T], xn[:, :, TP:T], amod[:, :, 1:9], ALU.mult))
                V.tensor_tensor(dst[:, :, TP:T], dst[:, :, TP:T], modT[:, shift:shift + KC, 1:9], ALU.add
                                ).then_inc(ev("h_ready"), 1)

            square("mix0", xn[:, :, :], xT[:, :, :])
            dve.wait_ge(ev("norm_sum"), NORM["mix0"])
            dve.nop().then_inc(ev("rows_used"), 1)
            for l in range(2):
                dve.wait_ge(ev("mod_turned"), l + 1)
                step(V.tensor_tensor(modT[:, 48 * l:48 * l + 48, :],
                                     ps[:, 6 + l, 0:432].rearrange("p (m n) -> p m n", n=9),
                                     rep(colA[:, 48 * l:48 * l + 48], 2, 9), ALU.add))
            dve.wait_ge(ev("mod_turned"), 3)
            V.tensor_tensor(modT[:, 96:112, :], ps[:, 0, 0:144].rearrange("p (m n) -> p m n", n=9),
                            rep(colA[:, 96:112], 2, 9), ALU.add).then_inc(ev("modkv"), 1)
            normalise("mix0")
            modulate("mix0", hT, B_MIX, 0, 8)

            dve.wait_ge(ev("gates"), 1)
            dve.wait_ge(ev("in_ml"), 64)
            step(V.tensor_scalar(gr[:, 0, 0:TP], ps[0:H, 4, 0:TP], small[0:H, 0:1], None, ALU.add))
            ch.mark(V.tensor_scalar(rowsS[:, 1, :], ps[0:H, 4, TP:T], small[0:H, 0:1], None, ALU.add))
            ch.mark(V.tensor_scalar(gr[:, 4, 0:TP], ps[0:H, 5, 0:TP], small[0:H, 1:2], None, ALU.add))
            step(V.tensor_scalar(rowsS[:, 5, :], ps[0:H, 5, TP:T], small[0:H, 1:2], None, ALU.add))
            ch.mark(V.scalar_tensor_tensor(out=rowsS[:, 2, :], in0=rowsS[:, 5, :], scalar=-1.0, in1=rowsS[:, 5, :],
                                           op0=ALU.mult, op1=ALU.max))
            V.scalar_tensor_tensor(out=gr[:, 1, 0:TP], in0=gr[:, 4, 0:TP], scalar=-1.0, in1=gr[:, 4, 0:TP],
                                   op0=ALU.mult, op1=ALU.max).then_inc(ev("gate_abs"), 1)
            dve.memset(scan[:, :, 0, 0:64], 0.0).then_inc(ev("scan_pad"), 1)
            dve.memset(scan[:, :, 1, 0:64], 0.0).then_inc(ev("scan_pad"), 1)
            dve.wait_ge(ev("gate_ln"), 1)
            dve.wait_ge(ev("scan_pad"), 2)
            cur = scan[:, :, 0, 64:192]
            step(V.scalar_tensor_tensor(out=cur, in0=gr[:, 4, 0:TP].rearrange("p (t n) -> p t n", t=2), scalar=0.0,
                                        in1=gr[:, 3, 0:TP].rearrange("p (t n) -> p t n", t=2),
                                        op0=ALU.min, op1=ALU.subtract))

            def scan_rows(op, at):
                s = 1
                while s < L:
                    step(V.tensor_tensor(scan[:, :, 1 - at, 64:192], scan[:, :, at, 64:192],
                                         scan[:, :, at, 64 - s:192 - s], op))
                    at, s = 1 - at, 2 * s
                return at

            at = scan_rows(ALU.add, 0)
            b_rows = gr[:, 6, :].rearrange("p (t n) -> p t n", t=2)
            u_rows = gr[:, 5, :].rearrange("p (t n) -> p t n", t=2)
            M_rows = gr[:, 8, :].rearrange("p (t n) -> p t n", t=2)
            m_rows = gr[:, 9, :].rearrange("p (t n) -> p t n", t=2)
            i_rows = gr[:, 0, :].rearrange("p (t n) -> p t n", t=2)
            step(V.tensor_copy(b_rows, scan[:, :, at, 64:192]))
            V.tensor_tensor(u_rows, i_rows, b_rows, ALU.subtract).then_inc(ev("rows_u"), 1)
            dve.wait_ge(ev("rows_u"), 1)
            ch.mark(V.memset(scan[:, :, 0, 0:64], -3e38))
            ch.mark(V.memset(scan[:, :, 1, 0:64], -3e38))
            step(V.tensor_copy(scan[:, :, 0, 64:192], u_rows))
            at = scan_rows(ALU.max, 0)
            step(V.tensor_scalar(M_rows[:, 0, :], scan[:, 0, at, 64:192], M_INIT, None, ALU.max))
            step(V.tensor_tensor(m_rows[:, 0, :], M_rows[:, 0, :], b_rows[:, 0, :], ALU.add))
            step(V.tensor_copy(small[0:H, 2:3], m_rows[:, 0, L - 1:L]))
            step(V.tensor_scalar(M_rows[:, 1, :], scan[:, 1, at, 64:192], small[0:H, 2:3], None, ALU.max))
            step(V.tensor_tensor(m_rows[:, 1, :], M_rows[:, 1, :], b_rows[:, 1, :], ALU.add))
            step(V.scalar_tensor_tensor(out=rowsS[:, 6, :], in0=rowsS[:, 5, :], scalar=0.0, in1=rowsS[:, 4, :],
                                        op0=ALU.min, op1=ALU.subtract))
            step(V.tensor_tensor(rowsS[:, 7, :], rowsS[:, 6, :], rowsS[:, 0, :], ALU.add))
            step(V.tensor_tensor(rowsS[:, 8, :], rowsS[:, 7, :], rowsS[:, 1, :], ALU.max))
            ch.mark(V.tensor_tensor(rowsS[:, 10, :], rowsS[:, 7, :], rowsS[:, 8, :], ALU.subtract))
            ch.mark(V.tensor_tensor(rowsS[:, 11, :], rowsS[:, 1, :], rowsS[:, 8, :], ALU.subtract))
            V.tensor_scalar(rowsS[:, 12, :], rowsS[:, 8, :], -1.0, None, ALU.mult).then_inc(ev("rows_m"), 1)

            dve.wait_ge(ev("u_ps"), 1)
            step(V.tensor_copy(small[:, 4:12], ps[:, 3, 0:8]))
            ch.mark(V.memset(v_tok[:, :, :, DV:VA], 1.0))
            nT = smp[:, 5, :]
            ch.mark(V.tensor_copy(nT, ps[:, 2, 300:332]))
            for g in range(6):
                dve.wait_ge(ev("kv_tok_ps"), g + 1)
                bank = ps[:, 4 + g % 4, :]
                if g < 2:
                    V.tensor_copy(k_tok[:, g, :], bank).then_inc(ev("kv_tok"), 1)
                else:
                    t, c = (g - 2) // 2, 2 * (g % 2)
                    V.tensor_copy(v_tok[:, t, c:c + 2, 0:DV], bank.rearrange("p (h n) -> p h n", n=DV)
                                  ).then_inc(ev("kv_tok"), 1)
            dve.wait_ge(ev("kv_tok"), 6)

            tri = cst[:, C_TRIU:C_TRIU + P]
            for h in range(H):
                dve.wait_ge(ev("head_tensor"), 3 * h + 1)
                if h:
                    dve.wait_ge(ev("head_tensor"), 3 * h)
                ch.mark(V.tensor_scalar(wmat[:, 0, :], ps[:, 0, 0:L], small[:, 4 + h:5 + h], 0.0,
                                        ALU.subtract, ALU.max))
                V.tensor_scalar(wmat[:, 1, :], ps[:, 0, L:2 * L], small[:, 8 + h:9 + h], 0.0,
                                ALU.subtract, ALU.max).then_inc(ev("head_vector"), 1)
                step(V.tensor_copy(small[:, 12:13], ps[:, 1, L - 1:L]))
                V.tensor_tensor(qw, projT[:, h, L:2 * L], ps[:, 1, 0:L], ALU.mult).then_inc(ev("head_vector"), 1)
                dve.wait_ge(ev("head_scalar"), 3 * h + 1)
                step(V.tensor_tensor(wmat, wmat, rep(tri, 1, 2), ALU.mult))
                ch.mark(V.tensor_scalar(ka[:, 0, :], k_tok[:, 0, h * DK:(h + 1) * DK], wmat[:, 0, L - 1:L], None, ALU.mult))
                V.tensor_scalar(ka[:, 1, :], k_tok[:, 1, h * DK:(h + 1) * DK], wmat[:, 1, L - 1:L], None, ALU.mult
                                ).then_inc(ev("head_vector"), 1)
                ch.mark(V.tensor_tensor(smat, ps[:, 2, 0:2 * L].rearrange("p (t n) -> p t n", t=2), wmat, ALU.mult))
                dve.wait_ge(ev("head_tensor"), 3 * h + 2)
                step(V.tensor_copy(c1, ps[:, 3, 0:VA]))
                V.tensor_scalar(nb, ones, c1[:, DV:VA], None, ALU.mult).then_inc(ev("head_vector"), 1)
                mem = xn[:, 2 * (h % 4):2 * (h % 4) + 2, :].rearrange("p c n -> p (c n)")[:, 0:VA]
                step(V.scalar_tensor_tensor(out=mem, in0=c1, scalar=small[:, 12:13], in1=ps[:, 4, 0:VA],
                                            op0=ALU.mult, op1=ALU.add))
                V.tensor_copy(small[:, 16 + h:17 + h], mem[:, DV:VA]).then_inc(ev("head_vector"), 1)
                dve.wait_ge(ev("head_scalar"), 3 * h + 2)
                dve.wait_ge(ev("head_tensor"), 3 * h + 3)
                step(V.tensor_scalar(mlx, ps[:, 6, 0:2 * L], -1.0, None, ALU.mult))
                step(V.tensor_tensor(mlx, mlx, ps[:, 6, 0:2 * L], ALU.max))
                step(V.tensor_tensor(mlx, mlx, enm, ALU.max))
                step(V.reciprocal(mlx, mlx))
                V.tensor_tensor(hh[:, 2 * h:2 * h + 2, 0:TP], ps[:, 5, :].rearrange("p (j n) -> p j n", j=2),
                                rep(mlx, 1, 2), ALU.mult).then_inc(ev("head_vector"), 1)

            qs = projT[:, 0:4, TP:T]
            ks = projT[:, 4:8, TP:T]
            vs = projT[:, 8:16, TP:T].rearrange("p (h j) b -> p h j b", j=2)
            sc_ = lambda r: smp[:, r, :].rearrange("p (h b) -> p h b", h=H)
            n_hb = nT.rearrange("p (b h) -> p h b", h=H)
            dve.wait_ge(ev("head_scalar"), 3 * H)
            wi, wa, em = bcs[:, :, 0:8], bcs[:, :, 8:16], bcs[:, :, 16:24]
            ch.mark(V.tensor_tensor(sc_(0), qs, ks, ALU.mult))
            V.tensor_tensor(sc_(1), qs, n_hb, ALU.mult).then_inc(ev("seq_prod"), 1)
            V.tensor_tensor(sc_(2), ks, wa, ALU.mult).then_inc(ev("seq_prod"), 1)
            dve.wait_ge(ev("seq_prod"), 2)
            step(V.tensor_tensor(sc_(3), n_hb, wi, ALU.mult))
            V.tensor_tensor(smp[:, 4, :].rearrange("p (b h) -> p h b", h=H), sc_(3), sc_(2), ALU.add
                            ).then_inc(ev("seq_prod"), 1)
            dve.wait_ge(ev("seq_ps"), 2)
            ch.mark(V.tensor_copy(k_row, ps[0:TS, 0, :]))
            ch.mark(V.tensor_copy(v_row[:, 0:512], ps[0:TS, 1, :]))
            step(V.tensor_copy(v_row[:, 512:1024], ps[0:TS, 2, :]))
            n = 0
            for b in range(TS):
                if b:
                    dve.wait_ge(ev("s_outer"), 4 * b)
                V.tensor_scalar(k_one, k_row, ident[0:TS, b:b + 1], None, ALU.mult).then_inc(ev("s_kone"), 1)
                dve.wait_ge(ev("s_qc"), b + 1)
                for h in range(H):
                    dve.wait_ge(ev("s_outer"), n + 1)
                    c = c_half[:, (b % 4) * H + h, :]
                    V.scalar_tensor_tensor(out=c, in0=c, scalar=bcs[:, h, b:b + 1], in1=ps[:, 3 + n % 2, 0:DV],
                                           op0=ALU.mult, op1=ALU.add).then_inc(ev("s_cnew"), 1)
                    n += 1
            dve.wait_ge(ev("seq_ps"), 1)
            dots = ps[:, 7, 0:64].rearrange("p (r h b) -> p r h b", r=2, h=H)
            ch.mark(V.tensor_tensor(sc_(6), dots[:, 0], wa, ALU.mult))
            step(V.tensor_tensor(sc_(7), dots[:, 1], wi, ALU.mult))
            step(V.tensor_tensor(sc_(7), sc_(7), sc_(6), ALU.add))
            step(V.tensor_scalar(sc_(8), sc_(7), -1.0, None, ALU.mult))
            step(V.tensor_tensor(sc_(8), sc_(8), sc_(7), ALU.max))
            step(V.tensor_tensor(sc_(8), sc_(8), em, ALU.max))
            step(V.reciprocal(sc_(8), sc_(8)))
            qc = ps[:, 7, 64:128].rearrange("p (h j b) -> p h j b", h=H, j=2)
            for j in range(2):
                ch.mark(V.tensor_tensor(sc_(10 + j), qc[:, :, j, :], wi, ALU.mult))
                step(V.tensor_tensor(sc_(12 + j), vs[:, :, j, :], sc_(6), ALU.mult))
                step(V.tensor_tensor(sc_(12 + j), sc_(12 + j), sc_(10 + j), ALU.add))
                step(V.tensor_tensor(hh.rearrange("p (h j) n -> p h j n", j=2)[:, :, j, TP:T], sc_(12 + j), sc_(8), ALU.mult))
            dve.wait_ge(ev("seq_ps"), 3)
            V.tensor_copy(nrow[0:H * TS, :], ps[0:H * TS, 5, 0:P]).then_inc(ev("n_rows"), 1)
            dve.wait_ge(ev("seq_ps"), 4)
            V.tensor_copy(small[0:H, 32:32 + P], ps[0:H, 6, 0:P]).then_inc(ev("n_rows"), 1)

            dve.wait_ge(ev("head_vector"), 6 * H)
            dve.wait_ge(ev("mem_stored"), 16 * H)
            square("head", xn[:, :, :], hh)
            og = projT[:, 16:24, :]
            step(V.tensor_scalar(og, og, 1.0, None, ALU.add))
            step(V.reciprocal(og, og))
            dve.wait_ge(ev("norm_rs"), NORM["head"])
            for h in range(H):
                ch.mark(V.tensor_tensor(hh[:, 2 * h:2 * h + 2, :], hh[:, 2 * h:2 * h + 2, :], rep(rs[:, h, :], 1, 2), ALU.mult))
            dve.wait_ge(ch.sem, ch.n)
            for c in range(KC):
                ins = V.scalar_tensor_tensor(out=hh[:, c, :], in0=hh[:, c, :], scalar=colB[:, B_HEAD + c:B_HEAD + c + 1],
                                             in1=og[:, c, :], op0=ALU.mult, op1=ALU.mult)
                if c < KC - 1:
                    ch.mark(ins)
            ins.then_inc(ev("mix_h"), 1)

            def add_gated(ph, half0, used0, gate, free):
                for m in range(KC):
                    dve.wait_ge(ev(("used" if m % 2 else "half") + ph), (used0 if m % 2 else half0) + m // 2 + 1)
                    o = ps[:, m % 2, :]
                    ch.mark(V.scalar_tensor_tensor(out=xT[:, m, 0:TP], in0=o[:, 0:TP], scalar=modT[:, gate + m, 0:1],
                                                   in1=xT[:, m, 0:TP], op0=ALU.mult, op1=ALU.add))
                    V.tensor_tensor(small[:, 200 + m * 8:208 + m * 8], o[:, TP:T], modT[:, gate + m, 1:9], ALU.mult
                                    ).then_inc(ev(free), 1)
                dve.wait_ge(ev(free), KC)
                step(V.tensor_tensor(xT[:, :, TP:T], xT[:, :, TP:T],
                                     small[:, 200:264].rearrange("p (c b) -> p c b", b=8), ALU.add))

            add_gated("A", 12, 2 * NADA + 20, 16, "x_out")
            square("ffn0", xn[:, :, :], xT[:, :, :])

            def moe_dve(l, ph):
                k0 = 48 * l
                ch.mark(V.memset(hT[:, :, T:TPAD], 0.0))
                normalise(f"ffn{l}")
                modulate(f"ffn{l}", hT, B_FFN + 8 * l, k0 + 24, k0 + 32)
                e3 = lambda r: rt[:, r]
                g3 = lambda v: v.rearrange("p t (g n) -> p t g n", n=8)
                dve.wait_ge(ev("sig_exp"), l + 1)
                step(V.tensor_scalar(e3(1), e3(0), 1.0, None, ALU.add))
                step(V.reciprocal(e3(1), e3(1)))
                step(V.tensor_tensor(e3(2), e3(1), rep(brt[:, l, :], 1, 3), ALU.add))
                for t in range(3):
                    for g in range(8):
                        ch.mark(V.max(g8[:, t, g, :], rt[:, 2, t, 8 * g:8 * g + 8]))
                step(V.memset(gsx[:, :, 8:12], NEG))
                step(V.tensor_tensor(gsx[:, :, 0:8], g8[:, :, :, 0], g8[:, :, :, 1], ALU.add))
                for t in range(3):
                    ch.mark(V.max(gs8[:, t, :], gsx[:, t, 0:8]))
                dve.wait_ge(ch.sem, ch.n)
                step(V.memset(gs8[:, :, 4:8], NEG))
                for t in range(3):
                    ch.mark(V.match_replace(gmk[:, t, :], gs8[:, t, :], gsx[:, t, :], 3e38))
                dve.wait_ge(ch.sem, ch.n)
                step(V.tensor_scalar(gsx[:, :, 0:8], gmk[:, :, 0:8], 3e38, None, ALU.is_equal))
                ch.mark(V.tensor_scalar(gs8[:, :, :], gsx[:, :, 0:8], -1.0, -NEG, ALU.add, ALU.mult))
                step(V.tensor_tensor(g3(e3(3)), g3(e3(2)), rep(gsx[:, :, 0:8], 3, 8), ALU.mult))
                step(V.tensor_tensor(g3(e3(3)), g3(e3(3)), rep(gs8, 3, 8), ALU.add))
                for t in range(3):
                    ch.mark(V.max(key8[:, t, :], rt[:, 3, t, :]))
                dve.wait_ge(ch.sem, ch.n)
                for t in range(3):
                    ch.mark(V.match_replace(rt[:, 4, t, :], key8[:, t, :], rt[:, 3, t, :], 3e38))
                dve.wait_ge(ch.sem, ch.n)
                step(V.tensor_scalar(e3(5), e3(4), 3e38, None, ALU.is_equal))
                for t in range(3):
                    V.tensor_scalar(rt[:, 7, t, :], rt[:, 5, t, :], cst[:, C_VALID + t:C_VALID + t + 1], None, ALU.mult
                                    ).then_inc(ev("mask"), 1)
                step(V.tensor_tensor(e3(6), e3(5), e3(1), ALU.mult))
                step(V.tensor_reduce(wsum[:, 0, :], e3(6), AX_X, ALU.add))
                step(V.reciprocal(wsum[:, 0, :], wsum[:, 0, :]))
                for t in range(3):
                    ch.mark(V.tensor_scalar(rt[:, 6, t, :], rt[:, 6, t, :], wsum[:, 0, t:t + 1], ROUTED_SCALE,
                                            ALU.mult, ALU.mult))
                dve.wait_ge(ev("route_ps"), 3 * l + 1)
                oc = over[:, P:P + 2]
                step(V.tensor_copy(oc[:, 0:1], ps[0:E, 7, 0:1]))
                step(V.tensor_scalar(oc[:, 1:2], oc[:, 0:1], float(SLOTS), None, ALU.is_gt))
                for j in range(2, 5):
                    step(V.scalar_tensor_tensor(out=oc[:, 1:2], in0=oc[:, 0:1], scalar=float(SLOTS * j), in1=oc[:, 1:2],
                                                op0=ALU.is_gt, op1=ALU.add))
                V.tensor_scalar(over[:, 0:P], ones[0:E, :], oc[:, 1:2], None, ALU.mult).then_inc(ev("route_in"), 1)
                dve.wait_ge(ev("used" + ph), sh_at[l] + 2)
                dve.wait_ge(ev("sh_silu"), 2 * l + 2)
                ch.mark(V.tensor_tensor(hs[:, 0, :], sgs[:, 0, :], ps[:, 5, 0:T], ALU.mult))
                V.tensor_tensor(hs[:, 1, :], sgs[:, 1, :], ps[:, 6, 0:T], ALU.mult).then_inc(ev("sh_hidden"), 1)
                dve.wait_ge(ev("route_ps"), 3 * l + 2)
                step(V.tensor_copy(oc[:, 0:1], ps[0:E, 7, 136:137]))
                V.tensor_scalar(cmp, cst[0:E, C_IOTA:C_IOTA + E], oc[:, 0:1], None, ALU.is_ge).then_inc(ev("route_in"), 1)
                nf = small[0:1, 400:401]
                step(V.tensor_scalar(nf, ps[0:1, 7, 137:138], 1.0, 1.0, ALU.max, ALU.add))
                step(V.tensor_copy(niter[0:1, l:l + 1], nf))
                step(V.tensor_scalar(niter[0:1, l:l + 1], niter[0:1, l:l + 1], 1, None, ALU.arith_shift_right))
                V.tensor_scalar(niter[0:1, l:l + 1], niter[0:1, l:l + 1], E // 2, None, ALU.add
                                ).then_inc(ev("table"), 1)
                iota3 = rep(cst[:, C_IOTA:C_IOTA + E], 1, 3)
                pos = ps[:, 0, 3 * E:6 * E].rearrange("p (t e) -> p t e", t=3)
                ch.mark(V.tensor_scalar(rt[:, 8, 0, :], cst[:, C_IOTA:C_IOTA + E], float(SLOTS), 1.0, ALU.mult, ALU.add))
                step(V.tensor_tensor(rt[:, 8, 1, :], ps[:, 7, 72:72 + E], cst[:, C_IOTA:C_IOTA + E], ALU.subtract))
                step(V.tensor_scalar(rt[:, 8, 1, :], rt[:, 8, 1, :], float(E - 1), float(SLOTS), ALU.add, ALU.mult))
                step(V.tensor_scalar(e3(9), pos, float(SLOTS), None, ALU.is_ge))
                step(V.tensor_tensor(e3(9), e3(9), rep(rt[:, 8, 1, :], 1, 3), ALU.mult))
                step(V.tensor_tensor(e3(9), e3(9), pos, ALU.add))
                step(V.tensor_tensor(e3(9), e3(9), rep(rt[:, 8, 0, :], 1, 3), ALU.add))
                step(V.tensor_tensor(e3(9), e3(9), e3(7), ALU.mult))
                for t in range(3):
                    ch.mark(V.max(key8[:, t, :], rt[:, 9, t, :]))
                dve.wait_ge(ch.sem, ch.n)
                step(V.tensor_scalar(place_f, key8, -1.0, None, ALU.add))
                step(V.tensor_copy(code_i, place_f))
                step(V.tensor_scalar(r_i, code_i, SLOTS - 1, None, ALU.bitwise_and))
                step(V.tensor_scalar(b_i, code_i, 6, None, ALU.arith_shift_right))
                step(V.scalar_tensor_tensor(out=place_f, in0=r_i, scalar=float(NBLK), in1=b_i, op0=ALU.mult, op1=ALU.add))
                V.tensor_copy(place_i, place_f).then_inc(ev("place"), 1)
                dve.wait_ge(ev("route_ps"), 3 * l + 3)
                step(V.tensor_scalar(small[0:1, 264:264 + E], ps[0:1, 3, 0:E], float(E - 1), None, ALU.min))
                V.tensor_copy(blk_e[0:1, l, :], small[0:1, 264:264 + E]).then_inc(ev("table"), 1)
                for m in range(KC):
                    if m < KC - 1:
                        dve.wait_ge(ev("sh_down"), 7 * l + m + 1)
                    else:
                        dve.wait_ge(ev("used" + ph), sh_at[l] + 3)
                    V.tensor_copy(shT[:, m, :], ps[:, 1 + m % 2, 0:T]).then_inc(ev("sh_out"), 1)
                for t in range(3):
                    for k in range(8):
                        step(V.scalar_tensor_tensor(out=rt[:, 10, t, :], in0=rt[:, 9, t, :], scalar=key8[:, t, k:k + 1],
                                                    in1=rt[:, 6, t, :], op0=ALU.is_equal, op1=ALU.mult,
                                                    accum_out=w8[:, t, k:k + 1]))

                dve.wait_ge(ev("table"), 2 * l + 2)
                n = dve.value_load(niter[0:1, l:l + 1], min_val=E // 2 + 1, max_val=(E + MAXOVER) // 2)
                dve.sem_inc(ev(f"hb{l}"), 2)
                dve.sem_inc(ev(f"xgT{l}"), 1)
                xg_cols = lambda u: xgT[:, u].rearrange("p c n -> p (c n)")
                dve.wait_ge(ev(f"xgT_ps{l}"), 2)
                V.tensor_copy(xg_cols(0), ps[:, 0, :]).then_inc(ev(f"xgT{l}"), 1)
                with dve.Fori(0, n) as i:
                    for u in range(2):
                        dve.wait_ge(ev(f"silu{l}"), i * 2 + (u + 1))
                        V.tensor_tensor(hb[:, u, :], sg[:, u, :], ps[:, 1 + u, 2 * SLOTS:4 * SLOTS], ALU.mult
                                        ).then_inc(ev(f"hb{l}"), 1)
                        dve.wait_ge(ev(f"xgT_ps{l}"), i * 2 + (u + 3))
                        V.tensor_copy(xg_cols(1 - u), ps[:, 0, :]).then_inc(ev(f"xgT{l}"), 1)

                for q in range(24):
                    t, k = divmod(q, 8)
                    n_t = P if t < 2 else TS
                    dve.wait_ge(ev(f"ycomb_{q % 4}"), 16 * (6 * l + q // 4 + 1))
                    if k == 0:
                        ins = V.tensor_scalar(acc[0:n_t, t, :], yk[0:n_t, q % 4, :], w8[0:n_t, t, k:k + 1], None, ALU.mult)
                    else:
                        dve.wait_ge(ev("acc"), 24 * l + q)
                        ins = V.scalar_tensor_tensor(out=acc[0:n_t, t, :], in0=yk[0:n_t, q % 4, :],
                                                     scalar=w8[0:n_t, t, k:k + 1], in1=acc[0:n_t, t, :],
                                                     op0=ALU.mult, op1=ALU.add)
                    ins.then_inc(ev("acc"), 1)
                for t in range(3):
                    dve.wait_ge(ev("accT"), 3 * l + t + 1)
                    if t < 2:
                        cols = slice(t * P, (t + 1) * P)
                        for g in range(2):
                            step(V.tensor_tensor(shT[:, 4 * g:4 * g + 4, cols], shT[:, 4 * g:4 * g + 4, cols],
                                                 ps[:, 2 * t + g, :].rearrange("p (c n) -> p c n", n=P), ALU.add))
                        for c in range(KC):
                            ch.mark(V.scalar_tensor_tensor(out=xT[:, c, cols], in0=shT[:, c, cols],
                                                           scalar=modT[:, k0 + 40 + c, 0:1], in1=xT[:, c, cols],
                                                           op0=ALU.mult, op1=ALU.add))
                    else:
                        step(V.tensor_tensor(shT[:, :, TP:T], shT[:, :, TP:T],
                                             ps[:, 4, 0:64].rearrange("p (c n) -> p c n", n=TS), ALU.add))
                        step(V.tensor_tensor(shT[:, :, TP:T], shT[:, :, TP:T], modT[:, k0 + 40:k0 + 48, 1:9], ALU.mult))
                        step(V.tensor_tensor(xT[:, :, TP:T], xT[:, :, TP:T], shT[:, :, TP:T], ALU.add))

            dve.wait_ge(ev("c_stored"), 32)
            dve.wait_ge(ev("stored"), 64)
            moe_dve(0, "A")

            square("mix1", xn[:, :, :], xT[:, :, :])
            dve.wait_ge(ev("pages"), 16 * TS)
            step(V.tensor_scalar(ptf, ptab, 8.0, cst[:, C_PMOD:C_PMOD + 1], ALU.mult, ALU.add))
            V.tensor_copy(cidx, ptf).then_inc(ev("cache_idx"), 1)
            normalise("mix1")
            modulate("kv", hkv, B_KV, 96, 104)
            dve.wait_ge(ev("h_ready"), H_READY["kv"])
            modulate("mix1", hT, B_MIX + 8, 48, 56)
            cos, sin = cst[0:ROPE, C_COS:C_COS + T], cst[0:ROPE, C_SIN:C_SIN + T]
            raw, sq = nq[:, 0], nq[:, 1]

            def raw_and_squares(tag, n):
                for c in range(n):
                    step(V.tensor_copy(raw[:, c, :], ps[:, c, 0:T]))
                V.tensor_tensor(sq[:, 0:n, :], raw[:, 0:n, :], raw[:, 0:n, :], ALU.mult).then_inc(ev("norm_sq"), 1)

            dve.wait_ge(ev("usedB"), 1)
            raw_and_squares("lat", 2)
            dve.wait_ge(ev("usedB"), 2)
            V.tensor_copy(krr, ps[0:ROPE, 4, 0:T]).then_inc(ev("kr_raw"), 1)
            dve.wait_ge(ev("norm_rs"), NORM["lat"])
            ch.mark(V.scalar_tensor_tensor(out=latT[:, 0, 0:T], in0=raw[:, 0, :], scalar=colB[:, B_LAT:B_LAT + 1],
                                           in1=rs[:, 0, :], op0=ALU.mult, op1=ALU.mult))
            V.scalar_tensor_tensor(out=latT[:, 1, 0:T], in0=raw[:, 1, :], scalar=colB[:, B_LAT + 1:B_LAT + 2],
                                   in1=rs[:, 0, :], op0=ALU.mult, op1=ALU.mult).then_inc(ev("lat_T"), 1)
            dve.wait_ge(ev("kr_rot"), 1)
            dve.wait_ge(ev("kr_raw"), 1)
            ch.mark(V.memset(latT[:, :, T:TPAD], 0.0))
            ch.mark(V.memset(krT[:, T:TPAD], 0.0))
            step(V.tensor_tensor(krT[:, 0:T], krr, cos, ALU.mult))
            step(V.tensor_tensor(krr, ps[0:ROPE, 4, 0:T], sin, ALU.mult))
            V.tensor_tensor(krT[:, 0:T], krT[:, 0:T], krr, ALU.add).then_inc(ev("kr_T"), 1)
            dve.wait_ge(ev("usedB"), 4)
            dve.wait_ge(ev("lat_T"), 1)
            raw_and_squares("ql", 3)
            dve.wait_ge(ev("norm_rs"), NORM["ql"])
            for c in range(3):
                ins = V.scalar_tensor_tensor(out=qlT[:, c, :], in0=raw[:, c, :], scalar=colB[:, B_QL + c:B_QL + c + 1],
                                             in1=rs[:, 0, :], op0=ALU.mult, op1=ALU.mult)
                if c < 2:
                    ch.mark(ins)
            ins.then_inc(ev("ql_T"), 1)
            for h in range(AH):
                if h % 3 == 2 or h == AH - 1:
                    dve.wait_ge(ev("usedB"), 4 + h // 3 + 1)
                else:
                    dve.wait_ge(ev("q_rope_ps"), h - h // 3 + 1)
                V.tensor_copy(qrope[:, h, :], ps[0:ROPE, 2 + h % 2, 0:T]).then_inc(ev("q_rope_raw"), 1)
            for h in range(AH):
                dve.wait_ge(ev("q_rot"), h + 1)
                V.tensor_tensor(hkv[0:ROPE, h, :], ps[0:ROPE, 4 + h % 4, 0:T], sin, ALU.mult).then_inc(ev("q_rot_out"), 1)
            step(V.tensor_tensor(qrope, qrope, rep(cos, 1, AH), ALU.mult))
            dve.wait_ge(ev("q_rot_out"), AH)
            V.tensor_tensor(qrope, qrope, hkv[0:ROPE], ALU.add).then_inc(ev("q_rope"), 1)

            caus = cst[:, C_CAUS:C_CAUS + P]
            for n in range(8):
                t, nk, u = n // 4, P * (n // 4 + 1), n % 2
                dve.wait_ge(ev("p_scores"), n + 1)
                bank = ps[:, u, :].rearrange("p (j k) -> p j k", j=2)
                if t:
                    ch.mark(V.tensor_scalar(s2[:, u, :, 0:P], bank[:, :, 0:P], ATT_SCALE, None, ALU.mult))
                V.scalar_tensor_tensor(out=s2[:, u, :, t * P:nk], in0=bank[:, :, t * P:nk], scalar=ATT_SCALE,
                                       in1=rep(caus, 1, 2), op0=ALU.mult, op1=ALU.add).then_inc(ev("unit_vector"), 1)
                dve.wait_ge(ev("unit_vector"), 4 * n + 1)
                step(V.tensor_reduce(att[:, 4 * u:4 * u + 2], s2[:, u, :, 0:nk], AX_X, ALU.max))
                V.tensor_scalar(att[:, 4 * u:4 * u + 2], att[:, 4 * u:4 * u + 2], -1.0, None, ALU.mult).then_inc(ev("unit_vector"), 1)
                dve.wait_ge(ev("unit_scalar"), 3 * n + 2)
                step(V.reciprocal(att[:, 4 * u + 2:4 * u + 4], att[:, 4 * u + 2:4 * u + 4]))
                V.tensor_tensor(s2[:, u, :, 0:nk], s2[:, u, :, 0:nk], rep(att[:, 4 * u + 2:4 * u + 4], 2, nk), ALU.mult
                                ).then_inc(ev("unit_vector"), 1)
                dve.wait_ge(ev("p_olat_ps"), n + 1)
                V.tensor_copy(qabs[:, :, 2 * (n % 4):2 * (n % 4) + 2, t * P:(t + 1) * P],
                              ps[:, 4 + u, :].rearrange("p (c j k) -> p c j k", c=2, j=2)).then_inc(ev("unit_vector"), 1)

            dve.sem_inc(ev("c_out_d"), 2)

            def cache_out(b, g):
                dve.wait_ge(ev("c_turned"), b * 12 + (g + 1))
                dst = latcT[:, g // 4, (g % 4) * 512:(g % 4 + 1) * 512] if g < 8 else krcT[:, (g - 8) * 512:(g - 7) * 512]
                src = ps[:, g % 4, :] if g < 8 else ps[0:ROPE, g % 4, :]
                V.tensor_copy(dst, src).then_inc(ev("c_out_d"), 1)

            SEQ_STEPS = 5

            def seq_dve(b, more):
                c2 = Chain(dve, ev("seq_steps"), b * SEQ_STEPS)
                dve.wait_ge(ev("seq_tensor"), b * 5 + 1)
                c2.mark(V.tensor_scalar(pss[:, 0:PAGES * AH], ps[:, 4, 0:PAGES * AH], ATT_SCALE, None, ALU.mult))
                selfm = (cst[:, C_SELF + b:C_SELF + b + 1] if isinstance(b, int)
                         else cst[:, bass.ds(b + C_SELF, 1)])
                c2.step(V.tensor_scalar(pss[:, PAGES * AH:], ps[:, 4, PAGES * AH:(PAGES + 1) * AH], ATT_SCALE, selfm,
                                        ALU.mult, ALU.add))
                by_head = pss.rearrange("p (t h) -> p h t", h=AH)
                V.tensor_reduce(att[:, 0:AH], by_head, AX_X, ALU.max).then_inc(ev("seq_vector"), 1)
                for g in (0, 2) if more else ():
                    cache_out(b + 1, g)
                dve.wait_ge(ev("seq_tensor"), b * 5 + 2)
                c2.step(V.tensor_reduce(att[0:AH, 24:25], ps[0:AH, 5, 0:P], AX_X, ALU.max))
                V.tensor_scalar(att[0:AH, 8:16], ident[0:AH, 0:AH], att[0:AH, 24:25], None, ALU.mult).then_inc(ev("seq_vector"), 1)
                for g in (4, 6) if more else ():
                    cache_out(b + 1, g)
                dve.wait_ge(ev("seq_tensor"), b * 5 + 3)
                V.tensor_tensor(pss.rearrange("p (t h) -> p t h", h=AH), pss.rearrange("p (t h) -> p t h", h=AH),
                                rep(ps[:, 5, 128:136], 1, PAGES + 1), ALU.subtract).then_inc(ev("seq_vector"), 1)
                for g in (8, 10) if more else ():
                    cache_out(b + 1, g)
                dve.wait_ge(ev("s_exp"), b + 1)
                V.tensor_reduce(att[:, 16:24], by_head, AX_X, ALU.add).then_inc(ev("seq_vector"), 1)
                dve.wait_ge(ev("seq_tensor"), b * 5 + 4)
                V.tensor_copy(att_row, ps[0:AH, 6, 0:CL]).then_inc(ev("att_row"), 1)
                dve.wait_ge(ev("seq_tensor"), b * 5 + 5)
                c2.step(V.reciprocal(att[:, 32:40], ps[:, 5, 136:144]))
                tok = slice(b + TP, b + TP + 1) if isinstance(b, int) else bass.ds(b + TP, 1)
                for c in range(2):
                    ins = V.tensor_tensor(qabs[:, c, :, tok].rearrange("p h o -> p (h o)"), ps[:, 6, CL + c * AH:CL + (c + 1) * AH], att[:, 32:40],
                                          ALU.mult)
                    if c == 0:
                        c2.mark(ins)
                ins.then_inc(ev("seq_vector"), 1)
                assert c2.n == SEQ_STEPS, c2.n

            for g in range(0, 12, 2):
                cache_out(0, g)
            with dve.Fori(0, 3) as i:
                for u in range(2):
                    seq_dve(i * 2 + u, True)
            seq_dve(6, True)
            seq_dve(7, False)
            add_gated("B", 0, 9, 64, "x1_out")
            square("ffn1", xn[:, :, :], xT[:, :, :])
            dve.wait_ge(ev("stored1"), 64)
            moe_dve(1, "B")
            square("fin", xn[:, :, :], xT[:, :, :])
            normalise("fin")
            for c in range(KC):
                ins = V.tensor_scalar(xn[:, c, :], xn[:, c, :], colB[:, B_FIN + c:B_FIN + c + 1], None, ALU.mult)
                if c < KC - 1:
                    ch.mark(ins)
            ins.then_inc(ev("y_T"), 1)
        @block.gpsimd
        def _(pool):
            def store(dst, src, what):
                pool.dma_start(dst, src).then_inc(ev(what), 16)

            pool.wait_ge(ev("zeros"), 1)
            pool.dma_start(slot_token.rearrange("(p b) o -> p (b o)", p=SLOTS), zero_i[:, :]).then_inc(ev("slots_zero"), 16)
            pool.wait_ge(ev("h_ready"), H_READY["mix0"])
            for v in range(2):
                pool.dma_start(y_slots[E * SLOTS:, v * 512:(v + 1) * 512].rearrange("(r p) n -> p r n", p=P),
                               rep(zero_row[:, :], 1, MAXOVER * SLOTS // P)).then_inc(ev("y_zero"), 16)
            for h in range(H):
                pool.wait_ge(ev("head_vector"), 6 * h + 5)
                mem = xn[:, 2 * h:2 * h + 2, :].rearrange("p c n -> p (c n)")
                store(o_pC[0, 0, h], mem[:, 0:DV], "mem_stored")
            with nc.allow_non_contiguous_dma(reason="a few numbers"):
                store(o_pm.rearrange("a b h -> h (a b)"), gr[:, 9, TP - 1:TP], "stored")
                store(o_sm[0].rearrange("b h -> h b"), rowsS[:, 8, :], "stored")
            c_dram = [w[0].rearrange("b h k v -> k (b h) v") for w in (a["state_mlstm_C"], o_sC)]
            pool.wait_ge(ev("s_cnew"), 16)
            store(c_dram[1][:, 0:16, :], c_half, "c_stored")
            pool.wait_ge(ev("c_stored"), 16)
            pool.dma_start(c_half, c_dram[0][:, 16:32, :]).then_inc(ev("in_c1"), 16)
            pool.wait_ge(ev("s_cnew"), 32)
            store(c_dram[1][:, 16:32, :], c_half, "c_stored")
            pool.wait_ge(ev("n_rows"), 1)
            store(o_sn[0].rearrange("b h k -> (b h) k"), nrow[0:H * TS, :], "stored")
            pool.wait_ge(ev("n_rows"), 2)
            store(o_pn[0, 0], small[0:H, 32:32 + P], "stored")

            def moe_pool(l):
                pool.wait_ge(ev("place"), l + 1)
                for t in range(3):
                    n_t = P if t < 2 else TS
                    for k in range(8):
                        nc.gpsimd.indirect_dma_start(
                            out=slot_token, out_offset=bass.IndirectOffsetOnAxis(ap=place_i[0:n_t, t, k:k + 1], axis=0),
                            in_=tok_i[0:n_t, t:t + 1], in_offset=None).then_inc(ev("placed"), 16)
                pool.wait_ge(ev("placed"), 384 * l + 24 * 16)
                pool.dma_start(idx_all, slot_token.rearrange("(p b) o -> p (b o)", p=SLOTS)).then_inc(ev("idx"), 16)
                pool.wait_ge(ev("idx"), 16 * l + 16)
                pool.wait_ge(ev("h_stored"), 48 * l + 48)

                def gather(u, b, count):
                    nc.gpsimd.tensor_copy(gidx[:, u:u + 1], idx_all[:, bass.ds(b, 1)]).then_inc(ev(f"gidx{l}"), 1)
                    pool.wait_ge(ev(f"gidx{l}"), count)
                    nc.gpsimd.nop(nofuse=True)
                    nc.gpsimd.indirect_dma_start(
                        out=xg[:, u, :], out_offset=None, in_=h_rows,
                        in_offset=bass.IndirectOffsetOnAxis(ap=gidx[:, u:u + 1], axis=0)).then_inc(ev(f"gath{l}_{u}"), 16)

                gather(0, 0, 1)
                n = pool.value_load(niter[0:1, l:l + 1], min_val=E // 2 + 1, max_val=(E + MAXOVER) // 2)
                with pool.Fori(0, n) as i:
                    for u in range(2):
                        pool.wait_ge(ev(f"xgT_ps{l}"), i * 2 + (u + 1))
                        gather(1 - u, i * 2 + (u + 1), i * 2 + (u + 2))
                for u in range(2):
                    pool.wait_ge(ev(f"y_stored{l}_{u}"), n * 16 + 16)
                nc.gpsimd.nop(nofuse=True)
                for q in range(24):
                    t, k = divmod(q, 8)
                    n_t = P if t < 2 else TS
                    if q >= 4:
                        pool.wait_ge(ev("acc"), 24 * l + q - 3)
                    nc.gpsimd.indirect_dma_start(
                        out=yk[0:n_t, q % 4, :], out_offset=None, in_=y_slots,
                        in_offset=bass.IndirectOffsetOnAxis(ap=code_i[0:n_t, t, k:k + 1], axis=0)
                    ).then_inc(ev(f"ycomb_{q % 4}"), 16)

            pool.wait_ge(ev("slots_zero"), 16)
            pool.wait_ge(ev("y_zero"), 32)
            pool.wait_ge(ev("table"), 2)
            moe_pool(0)

            pool.wait_ge(ev("norm_sq"), NORM["mix1"])
            with nc.allow_non_contiguous_dma(reason="the page table, each entry to eight partitions"):
                for b in range(TS):
                    pool.dma_start(ptab[:, b:b + 1], rep(a["page_table"][b], 1, 8)).then_inc(ev("pages"), 16)
            pool.wait_ge(ev("cache_idx"), 1)
            lat_rows = a["cache_latent"].rearrange("n (r t) c -> (n r) (t c)", r=8)
            kr_rows = a["cache_krope"].rearrange("n (r t) c -> (n r) (t c)", r=8)
            for b in range(TS):
                if b == 1:
                    pool.wait_ge(ev("q_abs_ps"), 2 * AH)
                if b >= 2:
                    pool.wait_ge(ev("seq_tensor"), 5 * (b - 2) + 4)
                for dst, src in ((latc, lat_rows), (krc, kr_rows)):
                    nc.gpsimd.indirect_dma_start(
                        out=dst[:, b % 2].rearrange("p t c -> p (t c)"), out_offset=None, in_=src,
                        in_offset=bass.IndirectOffsetOnAxis(ap=cidx[:, b:b + 1], axis=0)).then_inc(ev(f"cache{b % 2}"), 16)
                if b == 0:
                    pool.wait_ge(ev("lat_tok"), 4)
                    store(o_plat[0].rearrange("(t p) c -> p t c", p=P), lat_tok, "stored1")
                    store(o_pkr[0].rearrange("(t p) c -> p t c", p=P), kr_tok[:, 0:2, :], "stored1")
                    store(o_slat.rearrange("b s c -> (b s) c"), lat_new, "stored1")
                    store(o_skr.rearrange("b s c -> (b s) c"), kr_tok[0:TS, 2, :], "stored1")
            moe_pool(1)
            pool.wait_ge(ev("stored1"), 64)
            pool.wait_ge(ev("c_stored"), 32)
            pool.wait_ge(ev("mem_stored"), 16 * H)
            pool.wait_ge(ev("stored"), 16 * 4)


_INS = ["x_prompt", "x_sample", "state_mlstm_C", "state_mlstm_n", "state_mlstm_m", "cache_latent", "cache_krope",
        "page_table", "c_prompt", "c_sample", "w_ada", "b_ada", "g_mix", "g_ffn", "w_mlstm_in", "b_mlstm_gates",
        "g_mlstm_head", "w_mlstm_out", "w_ada_kv", "b_ada_kv", "g_kv_in", "w_dkv", "g_kv_lat", "w_uk", "w_uv",
        "w_dq", "g_q_lat", "w_uq", "w_mla_out", "w_router", "b_router", "w_exp_gate", "w_exp_up", "w_exp_down",
        "w_sh_gate", "w_sh_up", "w_sh_down", "g_final"]
_OUTS = [(1, TP, D), (TS, 1, D), (1, 1, H, DK, DV), (1, 1, H, DK), (1, 1, H), (1, TP, CL), (1, TP, ROPE),
         (1, TS, H, DK, DV), (1, TS, H, DK), (1, TS, H), (TS, 1, CL), (TS, 1, ROPE)]


def kernel(**inputs):
    import numpy as _np
    import concourse.bacc as _bacc
    from concourse import mybir as _mybir
    from concourse.bass_utils import run_bass_kernel_spmd as _run

    nc = _bacc.Bacc("TRN2", target_bir_lowering=False, num_devices=1)
    arrays, args = {}, {}
    given = dict(inputs, consts=constants())
    for name in _INS + ["consts"]:
        v = _np.ascontiguousarray(given[name])
        arrays[f"in_{name}_dram"] = v
        args[name] = nc.dram_tensor(f"in_{name}_dram", v.shape, _mybir.dt.from_np(v.dtype), kind="ExternalInput").ap()
    outs = [nc.dram_tensor(f"out_{i}_dram", shape, F32, kind="ExternalOutput").ap() for i, shape in enumerate(_OUTS)]
    decoder_step(nc, args, outs)
    r = _run(nc, [arrays], core_ids=[0])
    return tuple(r.results[0][f"out_{i}_dram"] for i in range(len(_OUTS)))
```
